# Optimizing a Trainium2 kernel written in Bass

```python
import math
import jax, jax.numpy as jnp
from jax import lax
import numpy as np

D_MODEL = 1024
BATCH = 1
SEQ = 512
DEPTH = 2

GRID_W = 64
CTX_LEN = 256
D_SSM = 512
D_FNET = 512
SSM_GROUP = 16
N_SSM_GROUPS = D_SSM // SSM_GROUP
STATE = 64
N_FNET_HEADS = 4
FNET_HEAD = D_FNET // N_FNET_HEADS
D_FF = 2816
N_MOD = 9
EPS = 1e-6
DT_MIN = 1e-3
DT_MAX = 1e-1
POS_BASE = 10000.0

kernel_name = "hybrid_s5_fnet_macaron_adaln_block"

def _rmsnorm(x, g):
    xf = x.astype(jnp.float32)
    y = xf * lax.rsqrt(jnp.mean(xf * xf, axis=-1, keepdims=True) + EPS)
    return (y * g.astype(jnp.float32)).astype(x.dtype)

def _pre(x, g, mod, k):
    return _rmsnorm(x, g) * (1.0 + mod[:, 3 * k + 1][:, None]) + mod[:, 3 * k][:, None]

def _post(x, y, g, mod, k, weight):
    return x + weight * mod[:, 3 * k + 2][:, None] * _rmsnorm(y, g)

def _swiglu(h, w_gu, w_down):
    gate, up = jnp.split(h @ w_gu, 2, axis=-1)
    return (jax.nn.silu(gate) * up) @ w_down

def _pos_2d(length, dtype):
    rows = length // GRID_W
    row = jnp.broadcast_to(jnp.arange(rows, dtype=jnp.float32)[:, None], (rows, GRID_W)).reshape(-1)
    col = jnp.broadcast_to(jnp.arange(GRID_W, dtype=jnp.float32)[None, :], (rows, GRID_W)).reshape(-1)
    quarter = D_MODEL // 4
    omega = 1.0 / (POS_BASE ** (jnp.arange(quarter, dtype=jnp.float32) / quarter))

    def enc(p):
        ang = p[:, None] * omega[None, :]
        return jnp.concatenate([jnp.sin(ang), jnp.cos(ang)], axis=-1)

    return jnp.concatenate([enc(row), enc(col)], axis=-1).astype(dtype)

def _scan_op(e1, e2):
    a1, b1 = e1
    a2, b2 = e2
    return a1 * a2, a2 * b1 + b2

def _discretize(lam_re, lam_im, log_dt, b_re, b_im, c_re, c_im):
    f32 = jnp.float32
    lam = lax.complex(lam_re.astype(f32), lam_im.astype(f32))
    dt = jnp.exp(log_dt.astype(f32))[:, None]
    lam_bar = jnp.exp(lam * dt)
    b = lax.complex(b_re.astype(f32), b_im.astype(f32))
    b_bar = ((lam_bar - 1.0) / lam)[..., None] * b
    c_mat = lax.complex(c_re.astype(f32), c_im.astype(f32))
    return lam_bar, b_bar, c_mat

def _s5_states(u, lam_bar, b_bar, s0):
    bu = jnp.einsum('gph,blgh->blgp', b_bar, u.astype(jnp.complex64))
    if s0 is not None:
        bu = bu.at[:, 0].add(lam_bar * s0)
    a = jnp.broadcast_to(lam_bar, bu.shape)
    _, xs = lax.associative_scan(_scan_op, (a, bu), axis=1)
    return xs

def _readout(c_mat, xs):
    return jnp.einsum('ghp,blgp->blgh', c_mat, xs).real

def _glu(y, w_glu):
    h = jax.nn.gelu(y)
    return h * jax.nn.sigmoid(h @ w_glu)

def _s5_mixer(u_lat, u_ctx, lam_re, lam_im, log_dt, b_re, b_im, c_re, c_im, d_skip, w_glu, need_ctx):
    bl, L, _ = u_lat.shape
    bc, Lc, _ = u_ctx.shape
    ul = u_lat.reshape(bl, L, N_SSM_GROUPS, SSM_GROUP)
    uc = u_ctx.reshape(bc, Lc, N_SSM_GROUPS, SSM_GROUP)
    y_lat = d_skip * u_lat
    y_ctx = d_skip * u_ctx if need_ctx else None
    for direction in range(2):
        lam_bar, b_bar, c_mat = _discretize(lam_re[direction], lam_im[direction], log_dt[direction],
                                            b_re[direction], b_im[direction], c_re[direction], c_im[direction])
        rev = direction == 1
        uc_d = jnp.flip(uc, axis=1) if rev else uc
        ul_d = jnp.flip(ul, axis=1) if rev else ul
        xs_c = _s5_states(uc_d, lam_bar, b_bar, None)
        xs_l = _s5_states(ul_d, lam_bar, b_bar, xs_c[:, -1])
        yl = _readout(c_mat, xs_l)
        if rev:
            yl = jnp.flip(yl, axis=1)
        y_lat = y_lat + yl.reshape(bl, L, D_SSM).astype(u_lat.dtype)
        if need_ctx:
            yc = _readout(c_mat, xs_c)
            if rev:
                yc = jnp.flip(yc, axis=1)
            y_ctx = y_ctx + yc.reshape(bc, Lc, D_SSM).astype(u_ctx.dtype)
    out_lat = _glu(y_lat, w_glu)
    out_ctx = _glu(y_ctx, w_glu) if need_ctx else None
    return out_lat, out_ctx

def _fnet(h, w_fmix):
    b, L, _ = h.shape
    hf = h.astype(jnp.float32).reshape(b, L, N_FNET_HEADS, FNET_HEAD)
    f = jnp.fft.fft2(hf, axes=(1, 3), norm="ortho").real.astype(h.dtype)
    return jnp.einsum('blnc,ncd->blnd', f, w_fmix).reshape(b, L, D_FNET)

def setup_inputs(seed: int = 0) -> dict:
    key = jax.random.key(seed)
    ks = jax.random.split(key, 24)
    f32 = jnp.float32
    D = D_MODEL
    G, P, H = N_SSM_GROUPS, STATE, SSM_GROUP
    nrm = lambda k, shape, s: jax.random.normal(k, shape, f32) * s
    n_idx = jnp.arange(P, dtype=f32)
    return {
        "x": nrm(ks[0], (BATCH, SEQ, D), 1.0),
        "c": nrm(ks[1], (BATCH, D), 1.0),
        "ctx": nrm(ks[2], (BATCH, CTX_LEN, D), 1.0),
        "c_ctx": nrm(ks[3], (D,), 1.0),
        "w_ada": nrm(ks[4], (DEPTH, D, N_MOD * D), 0.5 * D ** -0.5),
        "b_ada": nrm(ks[5], (DEPTH, N_MOD * D), 0.01),
        "norm_g": 1.0 + nrm(ks[6], (DEPTH, 6, D), 0.02),
        "ffn1_gu": nrm(ks[7], (DEPTH, D, 2 * D_FF), D ** -0.5),
        "ffn1_down": nrm(ks[8], (DEPTH, D_FF, D), D_FF ** -0.5),
        "ffn2_gu": nrm(ks[9], (DEPTH, D, 2 * D_FF), D ** -0.5),
        "ffn2_down": nrm(ks[10], (DEPTH, D_FF, D), D_FF ** -0.5),
        "w_in": nrm(ks[11], (DEPTH, D, D_SSM + D_FNET), D ** -0.5),
        "w_out": nrm(ks[12], (DEPTH, D_SSM + D_FNET, D), (D_SSM + D_FNET) ** -0.5),
        "ssm_lam_re": -0.5 + nrm(ks[13], (DEPTH, 2, G, P), 0.01),
        "ssm_lam_im": math.pi * n_idx + nrm(ks[14], (DEPTH, 2, G, P), 0.01),
        "ssm_log_dt": jax.random.uniform(ks[15], (DEPTH, 2, G), f32, math.log(DT_MIN), math.log(DT_MAX)),
        "ssm_b_re": nrm(ks[16], (DEPTH, 2, G, P, H), (2 * H) ** -0.5),
        "ssm_b_im": nrm(ks[17], (DEPTH, 2, G, P, H), (2 * H) ** -0.5),
        "ssm_c_re": nrm(ks[18], (DEPTH, 2, G, H, P), 2 ** -0.5),
        "ssm_c_im": nrm(ks[19], (DEPTH, 2, G, H, P), 2 ** -0.5),
        "ssm_d": nrm(ks[20], (DEPTH, D_SSM), 1.0),
        "w_glu": nrm(ks[21], (DEPTH, D_SSM, D_SSM), D_SSM ** -0.5),
        "w_fmix": nrm(ks[22], (DEPTH, N_FNET_HEADS, FNET_HEAD, FNET_HEAD), FNET_HEAD ** -0.5),
    }

def reference(x, c, ctx, c_ctx, w_ada, b_ada, norm_g, ffn1_gu, ffn1_down, ffn2_gu, ffn2_down,
              w_in, w_out, ssm_lam_re, ssm_lam_im, ssm_log_dt, ssm_b_re, ssm_b_im, ssm_c_re, ssm_c_im,
              ssm_d, w_glu, w_fmix):
    b, L, D = x.shape
    x = x + _pos_2d(L, x.dtype)[None]
    xc = ctx
    for l in range(DEPTH):
        last = l == DEPTH - 1
        mod_lat = (jax.nn.silu(c) @ w_ada[l] + b_ada[l]).reshape(b, N_MOD, D)
        mod_ctx = (jax.nn.silu(c_ctx) @ w_ada[l] + b_ada[l]).reshape(1, N_MOD, D)
        g = norm_g[l]
        x = _post(x, _swiglu(_pre(x, g[0], mod_lat, 0), ffn1_gu[l], ffn1_down[l]), g[1], mod_lat, 0, 0.5)
        xc = _post(xc, _swiglu(_pre(xc, g[0], mod_ctx, 0), ffn1_gu[l], ffn1_down[l]), g[1], mod_ctx, 0, 0.5)
        h = _pre(x, g[2], mod_lat, 1) @ w_in[l]
        hc = _pre(xc, g[2], mod_ctx, 1) @ w_in[l]
        y_ssm, yc_ssm = _s5_mixer(h[..., :D_SSM], hc[..., :D_SSM], ssm_lam_re[l], ssm_lam_im[l],
                                  ssm_log_dt[l], ssm_b_re[l], ssm_b_im[l], ssm_c_re[l], ssm_c_im[l],
                                  ssm_d[l], w_glu[l], not last)
        y_f = _fnet(h[..., D_SSM:], w_fmix[l])
        y = jnp.concatenate([y_ssm, y_f], axis=-1) @ w_out[l]
        x = _post(x, y, g[3], mod_lat, 1, 1.0)
        if not last:
            yc_f = _fnet(hc[..., D_SSM:], w_fmix[l])
            yc = jnp.concatenate([yc_ssm, yc_f], axis=-1) @ w_out[l]
            xc = _post(xc, yc, g[3], mod_ctx, 1, 1.0)
        x = _post(x, _swiglu(_pre(x, g[4], mod_lat, 2), ffn2_gu[l], ffn2_down[l]), g[5], mod_lat, 2, 0.5)
        if not last:
            xc = _post(xc, _swiglu(_pre(xc, g[4], mod_ctx, 2), ffn2_gu[l], ffn2_down[l]), g[5], mod_ctx, 2, 0.5)
    return x


_drawn_inputs = setup_inputs


def setup_inputs(seed=0):
    import zlib

    import numpy as np

    out = dict(_drawn_inputs(seed))
    spreads = {}
    factors = {'b_ada': 3.746, 'norm_g': 4.388, 'ssm_lam_re': 8.0}
    for name, (base, spread) in spreads.items():
        noise = np.random.default_rng([zlib.crc32(name.encode()), seed]).standard_normal(out[name].shape)
        drawn = base * np.exp(spread * noise) if base else spread * noise
        out[name] = __import__('jax').numpy.asarray(drawn.astype(out[name].dtype))
    for name, factor in factors.items():
        out[name] = (out[name] * factor).astype(out[name].dtype)
    return out
```

```python
import math
from contextlib import ExitStack

import numpy as np

import concourse.bass as bass
from concourse import mybir

DEPTH, D, SEQ, CTX = 2, 1024, 512, 256
TOK = SEQ + CTX
FF = 2816
KC = D // 128
FC = FF // 128
NMOD = 9
EPS = 1e-6
GRID_W = 64
DS = 512
HC = DS // 128
GH = 16
NST = 64
T8 = 8
NCH = TOK // T8
CCH = CTX // T8
NPAIR = 16
LD = 2 * NPAIR
QP = NPAIR // HC
QT = 2 * QP
QG = 2 * QP
STRIP = (2 * T8 - 1) * GH
NPIV = 7
RAW_SLOTS, SPLIT_SLOTS = 4, 3
RIDE = 3
TWO_PI = 2 * math.pi
MAGIC = 12582912.0
PI_A, PI_B = 6.28125, 0.0019350051879882812
PI_C = TWO_PI - PI_A - PI_B

f32, f32r = mybir.dt.float32, mybir.dt.float32r
ALU = mybir.AluOpType
ACT = mybir.ActivationFunctionType

LAT, CTXV = 0, 1


def token_segments(tok0):
    return [(CTX, TOK, LAT)] if tok0 else [(0, CTX, CTXV), (CTX, TOK, LAT)]


def build(nc, x, c, ctx_in, c_ctx, w_ada, b_ada, norm_g, ffn1_gu, ffn1_down, ffn2_gu, ffn2_down, w_in, w_out,
          lam_re, lam_im, log_dt, b_re, b_im, c_re, c_im, ssm_d, w_glu, w_fmix,
          pos_row, pos_col, dft_lat, dft_ctx, dft_head, out):
    stack = ExitStack()
    K = 1024
    BASE = 16512

    def sb(name, shape, kb, dt=f32):
        return nc.alloc_sbuf_tensor_at(name, shape, dt, offset=BASE + int(kb * K))

    def sem(name):
        return stack.enter_context(nc.semaphore(name))

    def scratch(name, shape):
        return nc.dram_tensor(name, shape, f32, kind="Internal").ap()

    xT = sb("xT", [128, KC, TOK], 0)
    hH = sb("hH", [128, KC, TOK], 24, f32r)
    hL = sb("hL", [128, KC, TOK], 48, f32r)
    raw = sb("raw", [128, RAW_SLOTS, 1024], 72)
    wH = sb("wH", [128, SPLIT_SLOTS, 1024], 88, f32r)
    wL = sb("wL", [128, SPLIT_SLOTS, 1024], 100, f32r)
    small = [112.0]

    def keep(name, shape):
        t = sb(name, shape, small[0])
        n = int(np.prod(shape[1:])) * 4
        small[0] += ((n + 31) // 32 * 32) / K
        return t

    modraw = keep("modraw", [128, DEPTH * NMOD * KC, 2])
    gT = keep("gT", [128, DEPTH * 6 * KC])
    adaB = keep("adaB", [128, DEPTH * NMOD * KC])
    ident = keep("ident", [128, 128])
    ones = keep("ones", [128, 8])
    siluC = keep("siluC", [128, KC, 2])
    skipD = keep("skipD", [128, DEPTH * HC])
    coefA = keep("coefA", [128, KC, 2])
    coefS = keep("coefS", [128, KC, 2])
    coefP = keep("coefP", [128, KC, 2])
    LkR = keep("LkR", [128, T8 + 1, 2 * LD])
    LkI = keep("LkI", [128, T8 + 1, 2 * LD])
    cfR = keep("cfR", [128, 2 * LD])
    cfI = keep("cfI", [128, 2 * LD])
    P8R = keep("P8R", [128, 2 * LD])
    P8I = keep("P8I", [128, 2 * LD])
    r8 = keep("r8", [128, 2 * LD])
    sumsq = keep("sumsq", [128, 8])
    rstd = keep("rstd", [128, 8])
    modrow = keep("modrow", [128, 128])
    assert small[0] <= 122, small[0]
    midH = sb("midH", [128, 4, TOK], 122, f32r)
    midL = sb("midL", [128, 4, TOK], 134, f32r)
    yT = sb("yT", [128, KC, TOK], 146)
    adaW = sb("adaW", [128, 2, KC, RIDE * 128], 170)
    sq = sb("sq", [128, KC, TOK], 170)
    sgate = sb("sgate", [128, 2, TOK], 194)
    midF = sb("midF", [128, 2, TOK], 200)
    tmpN = sb("tmpN", [128, 2, TOK], 200)
    sumY = sb("sumY", [128, TOK], 128)
    sumX = sb("sumX", [128, TOK], 131)
    xin = sb("xin", [128, 6, D], 146)
    prow = sb("prow", [128, 6, 128], 122)
    pdt = sb("pdt", [128, 4], 125)
    posR = sb("posR", [128, 4, SEQ // GRID_W], 125.25)
    posC = sb("posC", [128, 4, GRID_W], 125.5)
    lamT = sb("lamT", [128, 2, 128], 127)
    cT = sb("cT", [128, 2 * KC + DEPTH * HC], 128.25)
    lt = sb("lt", [128, 20, 2 * LD], 129)
    CTr = sb("CTr", [128, LD, GH], 122)
    CTi = sb("CTi", [128, LD, GH], 124)
    BbR = sb("BbR", [128, LD, GH], 126)
    BbI = sb("BbI", [128, LD, GH], 128)
    crow = sb("crow", [128, 2, 4, 128], 130)
    V = sb("V", [128, 2, QT, 128], 130)
    brow = sb("brow", [128, 2, LD, GH], 138)
    gt = sb("gt", [128, 2, QT, 128], 138)
    W = sb("W", [128, 2, QT, 128], 146)
    fmixW = sb("fmixW", [128, HC, 128], 154)
    headDft = sb("headDft", [128, 2, 128], 156)
    XF = sb("XF", [128, HC, TOK], 158)
    UP = sb("UP", [128, HC, T8, NCH], 170)
    VTm = sb("VTm", [128, 2, QT, 128], 182)
    strip = sb("strip", [16, QG, STRIP], 190)
    EG = sb("EG", [128, 2, QT, NCH], 198)
    et = sb("et", [128, 2, QT, 32], 204)
    pt = sb("pt", [128, 4, LD], 204)
    piv = sb("piv", [128, NPIV, 2, LD], 206)
    seqC = sb("seqC", [128, 4, SEQ], 24)
    ctxCS = sb("ctxCS", [128, 2, 2, CTX], 32)
    seqS = sb("seqS", [128, 4, SEQ], 48)
    CW = sb("CW", [128, HC, 2, 128], 56)
    PQ = sb("PQ", [128, 2, 6, 2, 128], 170)
    UP2 = sb("UP2", [128, HC, T8, NCH], 24)
    G = sb("G", [128, HC, TOK], 48)
    Ws, VTs, Tz, Es = [], [], [], []
    for s in range(2):
        o = 122 + 26 * s
        Ws.append(sb(f"Ws{s}", [128, 2, QT, 128], o))
        VTs.append(sb(f"VTs{s}", [128, 2, QT, 128], o + 8))
        Tz.append(sb(f"Tz{s}", [128, QG, 128], o + 16))
        Es.append(sb(f"Es{s}", [128, 2, QT, NCH], o + 20))
    UC = sb("UC", [128, 2, QG, NCH], 174)
    za, zb, zc, zd = (sb(n, [128, QT, NCH], 180 + 3 * i) for i, n in enumerate(["za", "zb", "zc", "zd"]))
    SR = sb("SR", [128, QT, NCH], 192)
    SI = sb("SI", [128, QT, NCH], 195)
    YC = sb("YC", [128, QG, NCH], 198)
    YP = sb("YP", [128, TOK], 201)
    gH = sb("gH", [128, HC, TOK], 122, f32r)
    gL = sb("gL", [128, HC, TOK], 134, f32r)
    zt = sb("zt", [128, 2, TOK], 180)
    sg2 = sb("sg2", [128, 2, TOK], 186)
    ostage = sb("ostage", [128, 4, D], 24)

    ps = stack.enter_context(nc.psum_tensor("ps", [128, 8, 512], f32))

    W_d = scratch("W_d", [DEPTH, HC, 128, 2 * QT * 128])
    VT_d = scratch("VT_d", [DEPTH, HC, 128, 2 * QT * 128])
    E_d = scratch("E_d", [DEPTH, HC, 128, 2 * QT * NCH])
    strip_d = scratch("strip_d", [DEPTH, HC, 16, QG * STRIP])
    u_d = scratch("u_d", [DEPTH, HC, 128, TOK])
    y_d = scratch("y_d", [DEPTH, HC, 128, QG * NCH])

    raw_ready = [sem(f"raw_ready{i}") for i in range(RAW_SLOTS)]
    w_hi = sem("w_hi")
    w_lo = sem("w_lo")
    w_used = sem("w_used")
    dve_chain, act_chain, pool_chain = sem("dve_chain"), sem("act_chain"), sem("pool_chain")
    counts = {"dve": 0, "act": 0, "pool": 0}

    def dlink(dve, ins):
        counts["dve"] += 1
        ins.then_inc(dve_chain, 1)

    def dsync(dve):
        dve.wait_ge(dve_chain, counts["dve"])

    def alink(act, ins):
        counts["act"] += 1
        ins.then_inc(act_chain, 1)

    def async_(act):
        act.wait_ge(act_chain, counts["act"])

    def plink(pool, ins):
        counts["pool"] += 1
        ins.then_inc(pool_chain, 1)
        pool.wait_ge(pool_chain, counts["pool"])

    ada_ready = [sem("ada_ready0"), sem("ada_ready1")]
    ada_used = sem("ada_used")
    ada_rows = sem("ada_rows")
    ada_turned = sem("ada_turned")
    ada_taken = sem("ada_taken")

    unit = 0

    NPH = FC // 2
    BODIES = (NPH - 1) // 2
    ROWS = 16 * (2 + 2 * 16 + 2)
    SET_A = 16 * (2 + T8)
    SET_C = 16 * (1 + T8)
    FFN_COUNTS = {"down_ready": (KC - 1) * NPH, "gate_read": FC, "up_read": FC, "down_read": KC * (NPH + 1),
                  "mid_hi": FC, "mid_lo": FC}
    MIX_COUNTS = {"proj_read": 8, "rows": ROWS, "ct_ps": 1, "ct": 1, "v_made": HC, "w_made": HC, "vt_ps": HC, "vt": HC,
                  "tz_ps": HC, "strip_taken": HC, "e_store": 16 * HC, "u_store": 16 * HC, "gen_store": 48 * HC, "dft": 48,
                  "cw_ps": 1, "cw": 1, "pq_ps": HC, "pq": HC, "f_ps": HC, "f_hi": HC, "f_lo": HC, "u_back": 16,
                  "b_ps": HC, "b_read": HC, "states": HC, "y_ps": HC, "y_taken": HC, "y_store": 16 * HC, "y_back": 16 * QG * HC,
                  "y_sum": HC, "gelu": HC, "g_hi": HC, "g_lo": HC, "glu_ps": 2, "sig": HC, "gated": HC, "cat_hi": HC,
                  "cat_lo": HC, "o_read": 8, "set_a": 2 * SET_A, "set_c": 2 * SET_C}
    down_ready = sem("down_ready")
    gate_read = sem("gate_read")
    up_read = sem("up_read")
    down_read = sem("down_read")
    mid_hi = sem("mid_hi")
    mid_lo = sem("mid_lo")
    sq_y = sem("sq_y")
    sum_y, all_y = sem("sum_y"), sem("all_y")
    ss_y = sem("ss_y")
    sd_y = sem("sd_y")
    rs_y = sem("rs_y")
    bc_y = sem("bc_y")
    x_new = sem("x_new")
    sq_x = sem("sq_x")
    sum_x, all_x = sem("sum_x"), sem("all_x")
    ss_x = sem("ss_x")
    sd_x = sem("sd_x")
    rs_x = sem("rs_x")
    bc_x = sem("bc_x")
    h_tmp = sem("h_tmp")
    h_hi = sem("h_hi")
    h_lo = sem("h_lo")
    proj_read = sem("proj_read")
    rows = sem("rows")
    ct_ps = sem("ct_ps")
    ct = sem("ct")
    v_made = sem("v_made")
    w_made = sem("w_made")
    vt_ps = sem("vt_ps")
    vt = sem("vt")
    tz_ps = sem("tz_ps")
    strip_taken = sem("strip_taken")
    e_store = sem("e_store")
    u_store = sem("u_store")
    gen_store = sem("gen_store")
    dft = sem("dft")
    cw_ps = sem("cw_ps")
    cw = sem("cw")
    pq_ps = sem("pq_ps")
    pq = sem("pq")
    f_ps = sem("f_ps")
    f_hi = sem("f_hi")
    f_lo = sem("f_lo")
    u_back = sem("u_back")
    b_ps = sem("b_ps")
    b_read = sem("b_read")
    states = sem("states")
    y_ps = sem("y_ps")
    y_taken = sem("y_taken")
    y_store = sem("y_store")
    y_back = sem("y_back")
    y_sum = sem("y_sum")
    gelu = sem("gelu")
    g_hi = sem("g_hi")
    g_lo = sem("g_lo")
    glu_ps = sem("glu_ps")
    sig = sem("sig")
    gated = sem("gated")
    cat_hi = sem("cat_hi")
    cat_lo = sem("cat_lo")
    o_read = sem("o_read")
    set_a = [sem("set_a0"), sem("set_a1")]
    set_c = [sem("set_c0"), sem("set_c1")]
    made = {"ffn": 0, "mix": 0, "post": 0, "pre": 0}

    class Section:

        def __init__(self, kind, totals):
            self.n0 = {n: made[kind] * totals[n] for n in totals}
            self.nth = made[kind]
            made[kind] += 1

    def make_ffn(tag, layer, gu, down, tok0, ride0):
        nonlocal unit
        F = Section("ffn", FFN_COUNTS)
        F.tag, F.layer, F.tok0, F.ride0, F.base = tag, layer, tok0, ride0, unit
        unit += 6 * (FC // 2)
        F.gu = gu[layer].rearrange("(k p) n -> p k n", p=128)
        F.down = down[layer].rearrange("(f p) n -> p f n", p=128)
        return F

    def make_norm(layer, k, tok0, weight):
        N = Section("post", {})
        N.layer, N.k, N.tok0, N.weight = layer, k, tok0, weight
        return N

    def make_pre(layer, k, tok0):
        N = Section("pre", {})
        N.layer, N.k, N.tok0 = layer, k, tok0
        return N

    def make_mixer(tag, layer):
        nonlocal unit
        M = Section("mix", MIX_COUNTS)
        M.tag, M.layer, M.base = tag, layer, unit
        unit += 8 + 2 + 8
        M.tok0 = CTX if layer == DEPTH - 1 else 0
        M.c0 = M.tok0 // T8
        return M

    pre_first = make_pre(0, 0, 0)
    F1 = [make_ffn(f"f1{l}", l, ffn1_gu, ffn1_down, 0, 8 if l == 0 else None) for l in range(1)]
    M0 = make_mixer("m0", 0)
    F2_0 = make_ffn("f20", 0, ffn2_gu, ffn2_down, 0, 28)
    F1_1 = make_ffn("f11", 1, ffn1_gu, ffn1_down, 0, None)
    M1 = make_mixer("m1", 1)
    F2_1 = make_ffn("f21", 1, ffn2_gu, ffn2_down, CTX, None)
    plan = []
    plan.append(("ffn", F1[0], make_norm(0, 0, 0, 0.5), make_pre(0, 1, 0)))
    plan.append(("mix", M0, make_norm(0, 1, 0, 1.0), make_pre(0, 2, 0)))
    plan.append(("ffn", F2_0, make_norm(0, 2, 0, 0.5), make_pre(1, 0, 0)))
    plan.append(("ffn", F1_1, make_norm(1, 0, 0, 0.5), make_pre(1, 1, 0)))
    plan.append(("mix", M1, make_norm(1, 1, CTX, 1.0), make_pre(1, 2, CTX)))
    plan.append(("ffn", F2_1, make_norm(1, 2, CTX, 0.5), None))
    pres = [pre_first] + [p[3] for p in plan[:-1]]
    NU = unit

    s_par, s_dt, s_xin, s_pos, s_id = sem("s_par"), sem("s_dt"), sem("s_xin"), sem("s_pos"), sem("s_id")
    s_exp, s_lam, s_parps, s_parT, s_silu, s_lamps = (sem("s_exp"), sem("s_lam"), sem("s_parps"), sem("s_parT"),
                                                      sem("s_silu"), sem("s_lamps"))
    s_xps, s_xctx, s_red, s_trig = sem("s_xps"), sem("s_xctx"), sem("s_red"), sem("s_trig")
    s_ops, s_ocp, s_out, s_xlat = sem("s_ops"), sem("s_ocp"), sem("s_out"), sem("s_xlat")

    def seg_ps(bank_ctx, bank_lat, vec):
        return ps[:, bank_lat, 0:SEQ] if vec == LAT else ps[:, bank_ctx, 0:CTX]

    def halves(tok0):
        return [(CTX, SEQ)] if tok0 else [(0, TOK // 2), (TOK // 2, TOK // 2)]

    def ps_pair(slot, tok0):
        return ps[:, 2 * slot, 0:SEQ] if tok0 else ps[:, 2 * slot:2 * slot + 2, 0:TOK // 2]

    def sb_pair(t, tok0):
        return t[:, CTX:TOK] if tok0 else t[:, 0:TOK].rearrange("p (h w) -> p h w", h=2)

    def load_unit(sp, i, r, F_base, src):
        n = F_base + i
        if n >= RAW_SLOTS:
            sp.wait_ge(w_lo, n - RAW_SLOTS + 1 + 12 * r)
        dst = raw[:, n % RAW_SLOTS, :]
        if len(src.shape) == 3:
            dst = dst.rearrange("p (k c) -> p k c", k=src.shape[1])
        sp.dma_start(dst, src).then_inc(raw_ready[n % RAW_SLOTS], 16)

    def split_hi(act, n, r=0):
        if isinstance(r, int) and n + 12 * r >= NU:
            return
        act.wait_ge(raw_ready[n % RAW_SLOTS], 16 * (n // RAW_SLOTS + 1) + 48 * r)
        if n >= SPLIT_SLOTS:
            act.wait_ge(w_used, n - SPLIT_SLOTS + 1 + 12 * r)
        nc.scalar.activation(wH[:, n % SPLIT_SLOTS, :], raw[:, n % RAW_SLOTS, :], ACT.Copy).then_inc(w_hi, 1)

    def split_lo(dve, n, r=0):
        if isinstance(r, int) and n + 12 * r >= NU:
            return
        dve.wait_ge(w_hi, n + 1 + 12 * r)
        nc.vector.tensor_tensor(wL[:, n % SPLIT_SLOTS, :], raw[:, n % RAW_SLOTS, :],
                                wH[:, n % SPLIT_SLOTS, :].bitcast(f32), ALU.subtract).then_inc(w_lo, 1)

    def three(pairs, dst, first, last):
        n = 0
        for wh, wl, xh, xl in pairs:
            for a, b in ((wh, xh), (wh, xl), (wl, xh)):
                ins = nc.tensor.matmul(dst, a, b, start=first and n == 0, stop=last and n == 3 * len(pairs) - 1)
                n += 1
        return ins

    def project(tok0, slot, wpairs, xh, xl, shift=0):
        for i, (t0, w) in enumerate(halves(tok0)):
            t0 -= shift
            ins = three([(a, b, xh[:, k, t0:t0 + w], xl[:, k, t0:t0 + w]) for k, (a, b) in enumerate(wpairs)],
                        ps[:, 2 * slot + i, 0:w], True, True)
        return ins

    def wtile(n, cols=128):
        s = n % SPLIT_SLOTS
        return (wH[:, s, :].rearrange("p (k c) -> p k c", c=cols), wL[:, s, :].rearrange("p (k c) -> p k c", c=cols))


    def ffn_sync(sp, F):
        def gate_up(f, i, r):
            load_unit(sp, i, r, F.base, F.gu[:, :, bass.ds(f * 128, 128)])
            load_unit(sp, i + 1, r, F.base, F.gu[:, :, bass.ds(f * 128 + FF, 128)])

        def body(r):
            for q in range(2):
                gate_up(4 * r + 2 * q + 2, 4 + 6 * q, r)
                gate_up(4 * r + 2 * q + 3, 6 + 6 * q, r)
                for j in range(2):
                    load_unit(sp, 8 + 6 * q + j, r, F.base, F.down[:, 4 * r + 2 * q + j, :])

        gate_up(0, 0, 0)
        gate_up(1, 2, 0)
        with sp.Fori(0, BODIES) as r:
            body(r)
        for j in range(2):
            load_unit(sp, 4 + 12 * BODIES + j, 0, F.base, F.down[:, FC - 2 + j, :])

    def ada_dma(pool, R, r, layer, ride_in_layer):
        if R >= 2:
            pool.wait_ge(ada_used, R - 1 + 4 * r)
        src = w_ada[layer].rearrange("(k p) n -> p k n", p=128)
        pool.dma_start(adaW[:, R % 2, :, :],
                       src[:, :, bass.ds(ride_in_layer * (RIDE * 128), RIDE * 128)]).then_inc(ada_ready[R % 2], 16)

    RIDES = NMOD * KC // RIDE

    def ffn_pool(pool, F, pre):
        if F.ride0 is None:
            return
        pool.wait_ge(h_lo, KC * pre.nth + KC)
        layer, first = divmod(F.ride0, RIDES)
        with pool.Fori(0, BODIES - 1) as r:
            for g in range(4):
                ada_dma(pool, F.ride0 + g, r, layer, first + g + 4 * r)
        for g in range(4):
            R = F.ride0 + 4 * (BODIES - 1) + g
            ada_dma(pool, R, 0, *divmod(R, RIDES))

    def ada_ride(pe, R, r, bank, col):
        pe.wait_ge(ada_ready[R % 2], 16 * (R // 2 + 1) + 32 * r)
        for j in range(RIDE):
            for k in range(KC):
                ins = nc.tensor.matmul(ps[32 * j:32 * j + 2, bank, col:col + 128], siluC[:, k, :],
                                       adaW[:, R % 2, k, j * 128:(j + 1) * 128], start=k == 0, stop=k == KC - 1)
        ins.then_inc(ada_used, 1)

    def ada_turn(pe, R, r, bank, col):
        pe.wait_ge(ada_rows, R + 1 + 4 * r)
        nc.tensor.transpose(ps[:, bank, col:col + 128], modrow[:], ident[:]).then_inc(ada_turned, 1)

    def take_rows(act, R, r, bank, col):
        act.wait_ge(ada_used, R + 1 + 4 * r)
        if R >= 1:
            act.wait_ge(ada_turned, R + 4 * r)
        else:
            act.wait_ge(s_id, 5)
        for j in range(RIDE):
            ins = nc.scalar.activation(modrow[32 * j:32 * j + 2, :], ps[32 * j:32 * j + 2, bank, col:col + 128], ACT.Copy)
        ins.then_inc(ada_rows, 1)

    def take_columns(act, R, r, bank, col):
        act.wait_ge(ada_turned, R + 1 + 4 * r)
        nc.scalar.activation(modraw[:, bass.ds(R * RIDE + 4 * RIDE * r, RIDE), :],
                             ps[:, bank, col:col + 32 * RIDE].rearrange("p (a b) -> p a b", b=32)[:, :, 0:2], ACT.Copy)\
            .then_inc(ada_taken, 1)

    def ffn_tensor(pe, F, pre):
        def gate_up(i, r, j, later, ride):
            for u in range(2):
                if later is not None:
                    pe.wait_ge(down_read, F.n0["down_read"] + later + 5 + 2 * j + u + 16 * r)
                    if u == 0:
                        pe.wait_ge(gate_read, F.n0["gate_read"] + later // 4 + j + 1 + 4 * r)
                    else:
                        pe.wait_ge(up_read, F.n0["up_read"] + later // 4 + j + 1 + 4 * r)
                if ride is not None and u == 0:
                    ada_turn(pe, ride - 1, r, 4 * j + 1, TOK // 2)
                    ada_ride(pe, ride, r, 4 * j, TOK // 2)
                n = F.base + i + u
                pe.wait_ge(w_lo, n + 1 + 12 * r)
                wh, wl = wtile(n)
                project(F.tok0, 2 * j + u, [(wh[:, k, :], wl[:, k, :]) for k in range(KC)], hH, hL)\
                    .then_inc(w_used, 1)

        def down(i, r, p, last):
            n = F.base + i
            pe.wait_ge(w_lo, n + 2 + 12 * r)
            pe.wait_ge(mid_lo, F.n0["mid_lo"] + 2 * p + 2 + 4 * r)
            (ah, al), (bh, bl) = wtile(n), wtile(n + 1)
            s0 = (2 * p) % 4
            for m in range(KC):
                if last or m >= 4:
                    pe.wait_ge(down_read, F.n0["down_read"] + 8 * (p + 1) - 3 + m + 16 * r)
                elif m % 2 == 0:
                    pe.wait_ge(gate_read, F.n0["gate_read"] + 2 * (p + 1) + m // 2 + 1 + 4 * r)
                else:
                    pe.wait_ge(up_read, F.n0["up_read"] + 2 * (p + 1) + m // 2 + 1 + 4 * r)
                for h, (t0, w) in enumerate(halves(F.tok0)):
                    ins = three([(ah[:, m, :], al[:, m, :], midH[:, s0, t0:t0 + w], midL[:, s0, t0:t0 + w]),
                                 (bh[:, m, :], bl[:, m, :], midH[:, s0 + 1, t0:t0 + w], midL[:, s0 + 1, t0:t0 + w])],
                                ps[:, 2 * (m % 4) + h, 0:w], True, True)
                if m < KC - 1:
                    ins.then_inc(down_ready, 1)
            ins.then_inc(w_used, 2)

        pe.wait_ge(h_lo, KC * pre.nth + KC)
        for j in range(2):
            gate_up(2 * j, 0, j, None, None)
        with pe.Fori(0, BODIES) as r:
            for q in range(2):
                for j in range(2):
                    gate_up(4 + 6 * q + 2 * j, r, j, 8 * q, None if F.ride0 is None else F.ride0 + 2 * q + j)
                down(8 + 6 * q, r, q, False)
        if F.ride0 is not None and F.ride0 + 4 * BODIES == 2 * RIDES:
            pe.wait_ge(down_read, F.n0["down_read"] + KC * NPH - 3)
            ada_turn(pe, 2 * RIDES - 1, 0, 1, TOK // 2)
            pe.wait_ge(ada_taken, 2 * RIDES)
        down(4 + 12 * BODIES, 0, NPH - 1, True)

    def loop(eng, F, body):
        n = BODIES - 1 if F.base + 6 * NPH == NU else BODIES
        with eng.Fori(0, n) as r:
            body(r)
        if n < BODIES:
            body(n)

    def ffn_scalar(act, F):
        def gate(i, r, f, ride):
            act.wait_ge(w_used, F.base + i + 1 + 12 * r)
            if ride is not None:
                take_columns(act, ride - 1, r, 4 * (f % 2) + 1, TOK // 2)
                take_rows(act, ride, r, 4 * (f % 2), TOK // 2)
            if f >= 2:
                act.wait_ge(up_read, F.n0["up_read"] + f - 1 + 4 * r)
            nc.scalar.activation(sb_pair(sgate[:, f % 2, :], F.tok0), ps_pair(2 * (f % 2), F.tok0), ACT.Silu)\
                .then_inc(gate_read, 1)
            split_hi(act, F.base + i + 3, r)

        def up(i, r, f):
            act.wait_ge(up_read, F.n0["up_read"] + f + 1 + 4 * r)
            nc.scalar.activation(midH[:, f % 4, F.tok0:TOK], midF[:, f % 2, F.tok0:TOK], ACT.Copy).then_inc(mid_hi, 1)
            split_hi(act, F.base + i + 3, r)

        for j in range(2):
            gate(2 * j, 0, j, None)
            up(2 * j + 1, 0, j)
        def body(r):
            for q in range(2):
                for j in range(2):
                    i, f = 4 + 6 * q + 2 * j, 2 + 2 * q + j
                    gate(i, r, f, None if F.ride0 is None else F.ride0 + 2 * q + j)
                    up(i + 1, r, f)
                split_hi(act, F.base + 8 + 6 * q + 3, r)
                split_hi(act, F.base + 9 + 6 * q + 3, r)

        loop(act, F, body)
        if F.ride0 is not None and F.ride0 + 4 * BODIES == 2 * RIDES:
            take_columns(act, 2 * RIDES - 1, 0, 1, TOK // 2)
        for j in range(2):
            split_hi(act, F.base + 4 + 12 * BODIES + j + 3)

    def ffn_vector(dve, F):
        for m in range(KC):
            nc.vector.memset(yT[:, m, F.tok0:TOK], 0.0).then_inc(down_read, 1)

        def up(i, r, f):
            dve.wait_ge(w_used, F.base + i + 1 + 12 * r)
            dve.wait_ge(gate_read, F.n0["gate_read"] + f + 1 + 4 * r)
            if f >= 2:
                dve.wait_ge(mid_hi, F.n0["mid_hi"] + f - 1 + 4 * r)
                dve.wait_ge(mid_lo, F.n0["mid_lo"] + f - 1 + 4 * r)
            nc.vector.tensor_tensor(sb_pair(midF[:, f % 2, :], F.tok0), ps_pair(2 * (f % 2) + 1, F.tok0),
                                    sb_pair(sgate[:, f % 2, :], F.tok0), ALU.mult).then_inc(up_read, 1)
            split_lo(dve, F.base + i + 3, r)
            dve.wait_ge(mid_hi, F.n0["mid_hi"] + f + 1 + 4 * r)
            nc.vector.tensor_tensor(midL[:, f % 4, F.tok0:TOK], midF[:, f % 2, F.tok0:TOK],
                                    midH[:, f % 4, F.tok0:TOK].bitcast(f32), ALU.subtract).then_inc(mid_lo, 1)

        def down(i, r, p):
            for m in range(KC):
                if m < KC - 1:
                    dve.wait_ge(down_ready, F.n0["down_ready"] + 7 * p + m + 1 + 14 * r)
                else:
                    dve.wait_ge(w_used, F.base + i + 2 + 12 * r)
                dve.wait_ge(down_read, F.n0["down_read"] + 8 * p + m + 1 + 16 * r)
                nc.vector.tensor_tensor(sb_pair(yT[:, m, :], F.tok0), ps_pair(m % 4, F.tok0),
                                        sb_pair(yT[:, m, :], F.tok0), ALU.add).then_inc(down_read, 1)
            split_lo(dve, F.base + i + 3, r)
            split_lo(dve, F.base + i + 4, r)

        for j in range(2):
            split_lo(dve, F.base + 2 * j + 3)
            up(2 * j + 1, 0, j)
        def body(r):
            for q in range(2):
                for j in range(2):
                    i, f = 4 + 6 * q + 2 * j, 2 + 2 * q + j
                    split_lo(dve, F.base + i + 3, r)
                    up(i + 1, r, f)
                down(8 + 6 * q, r, q)

        loop(dve, F, body)
        down(4 + 12 * BODIES, 0, NPH - 1)

    def y_ready(eng, S, m):
        if S.tag.startswith("f"):
            eng.wait_ge(down_read, S.n0["down_read"] + KC * NPH + m + 1)
        else:
            eng.wait_ge(o_read, S.n0["o_read"] + m + 1)

    def add_squares(pool, N, squares, acc, done):
        for m in range(1, KC - 1):
            pool.wait_ge(squares, KC * N.nth + m + 1)
            ins = nc.gpsimd.tensor_tensor(acc[:, N.tok0:TOK], (sq[:, 0] if m == 1 else acc)[:, N.tok0:TOK],
                                          sq[:, m, N.tok0:TOK], ALU.add)
            if m < KC - 2:
                plink(pool, ins)
        ins.then_inc(done, 1)

    def add_last_squares(dve, N, squares, acc, summed, done):
        dve.wait_ge(summed, N.nth + 1)
        dve.wait_ge(squares, KC * N.nth + KC)
        nc.vector.tensor_tensor(acc[:, N.tok0:TOK], acc[:, N.tok0:TOK], sq[:, KC - 1, N.tok0:TOK], ALU.add)\
            .then_inc(done, 1)

    def stat_matmuls(pe, acc, bank, tok0):
        for b in range(tok0 // 128, TOK // 128):
            ins = nc.tensor.matmul(ps[:, bank, b:b + 1], acc[:, b * 128:(b + 1) * 128], ones[:, 0:1],
                                   start=True, stop=True)
        return ins

    def spread_matmuls(pe, bank_ctx, bank_lat, tok0):
        for b in range(tok0 // 128, TOK // 128):
            bank, col = (bank_ctx, b * 128) if b < 2 else (bank_lat, b * 128 - CTX)
            ins = nc.tensor.matmul(ps[:, bank, col:col + 128], rstd[:, b:b + 1].broadcast_to([128, 128]), ident[:],
                                   start=True, stop=True)
        return ins

    def post_tensor(pe, N, S):
        pe.wait_ge(all_y, N.nth + 1)
        stat_matmuls(pe, sumY, 0, N.tok0).then_inc(ss_y, 1)
        pe.wait_ge(rs_y, N.nth + 1)
        spread_matmuls(pe, 2, 3, N.tok0).then_inc(bc_y, 1)

    def pre_tensor(pe, N):
        pe.wait_ge(all_x, N.nth + 1)
        stat_matmuls(pe, sumX, 1, N.tok0).then_inc(ss_x, 1)
        pe.wait_ge(rs_x, N.nth + 1)
        spread_matmuls(pe, 6, 7, N.tok0).then_inc(bc_x, 1)

    def root(act, bank, tok0, nth, ready, done):
        b = tok0 // 128
        act.wait_ge(ready, nth + 1)
        nc.scalar.activation(sumsq[:, b:6], ps[:, bank, b:6], ACT.Sqrt, bias=ones[:, 1:2], scale=1.0 / D).then_inc(done, 1)

    def post_scalar(act, N, S):
        for m in range(KC):
            y_ready(act, S, m)
            nc.scalar.activation(sq[:, m, N.tok0:TOK], yT[:, m, N.tok0:TOK], ACT.Square).then_inc(sq_y, 1)
        root(act, 0, N.tok0, N.nth, ss_y, sd_y)

    def pre_scalar(act, N, x_new, before):
        for m in range(KC):
            act.wait_ge(x_new, before + m + 1)
            nc.scalar.activation(sq[:, m, N.tok0:TOK], xT[:, m, N.tok0:TOK], ACT.Square).then_inc(sq_x, 1)
        root(act, 1, N.tok0, N.nth, ss_x, sd_x)
        for m in range(KC):
            act.wait_ge(h_tmp, KC * N.nth + m + 1)
            for t0, t1, v in token_segments(N.tok0):
                ins = nc.scalar.activation(hH[:, m, t0:t1], tmpN[:, m % 2, t0:t1], ACT.Identity,
                                           bias=coefS[:, m, v:v + 1])
            ins.then_inc(h_hi, 1)

    def mod_chunk(layer, i):
        at = (layer * NMOD + i) * KC
        return modraw[:, at:at + KC, :], adaB[:, at:at + KC].unsqueeze(2).broadcast_to([128, KC, 2])

    def g_chunk(layer, i):
        at = (layer * 6 + i) * KC
        return gT[:, at:at + KC].unsqueeze(2).broadcast_to([128, KC, 2])

    def coef_post(dve, N):
        a, b = mod_chunk(N.layer, 3 * N.k + 2)
        dlink(dve, nc.vector.tensor_tensor(coefP[:], a, b, ALU.add))
        dsync(dve)
        dlink(dve, nc.vector.scalar_tensor_tensor(coefP[:], coefP[:], N.weight, g_chunk(N.layer, 2 * N.k + 1),
                                                  ALU.mult, ALU.mult))

    def coef_pre(dve, N):
        a, b = mod_chunk(N.layer, 3 * N.k + 1)
        dlink(dve, nc.vector.tensor_tensor(coefA[:], a, b, ALU.add))
        dsync(dve)
        dlink(dve, nc.vector.scalar_tensor_tensor(coefA[:], coefA[:], 1.0, g_chunk(N.layer, 2 * N.k), ALU.add, ALU.mult))
        a, b = mod_chunk(N.layer, 3 * N.k)
        dlink(dve, nc.vector.tensor_tensor(coefS[:], a, b, ALU.add))

    def inverse(dve, tok0, nth, ready, done):
        b = tok0 // 128
        dve.wait_ge(ready, nth + 1)
        nc.vector.reciprocal(rstd[:, b:6], sumsq[:, b:6]).then_inc(done, 1)

    def post_vector(dve, N):
        coef_post(dve, N)
        add_last_squares(dve, N, sq_y, sumY, sum_y, all_y)
        inverse(dve, N.tok0, N.nth, sd_y, rs_y)
        dve.wait_ge(bc_y, N.nth + 1)
        for m in range(KC):
            if m == 0:
                dsync(dve)
            if m >= 2:
                dve.wait_ge(x_new, KC * N.nth + m - 1)
            for t0, t1, v in token_segments(N.tok0):
                dlink(dve, nc.vector.scalar_tensor_tensor(tmpN[:, m % 2, t0:t1], yT[:, m, t0:t1], coefP[:, m, v:v + 1],
                                                          seg_ps(2, 3, v), ALU.mult, ALU.mult))
            dsync(dve)
            nc.vector.tensor_tensor(xT[:, m, N.tok0:TOK], xT[:, m, N.tok0:TOK], tmpN[:, m % 2, N.tok0:TOK], ALU.add)\
                .then_inc(x_new, 1)

    def pre_vector(dve, N):
        coef_pre(dve, N)
        add_last_squares(dve, N, sq_x, sumX, sum_x, all_x)
        inverse(dve, N.tok0, N.nth, sd_x, rs_x)
        dve.wait_ge(bc_x, N.nth + 1)
        dsync(dve)

        def rest(m):
            dve.wait_ge(h_hi, KC * N.nth + m + 1)
            for t0, t1, v in token_segments(N.tok0):
                ins = nc.vector.scalar_tensor_tensor(hL[:, m, t0:t1], tmpN[:, m % 2, t0:t1], coefS[:, m, v:v + 1],
                                                     hH[:, m, t0:t1].bitcast(f32), ALU.add, ALU.subtract)
            ins.then_inc(h_lo, 1)

        for m in range(KC):
            if m >= 2:
                dve.wait_ge(h_lo, KC * N.nth + m - 1)
            for t0, t1, v in token_segments(N.tok0):
                ins = nc.vector.scalar_tensor_tensor(tmpN[:, m % 2, t0:t1], xT[:, m, t0:t1], coefA[:, m, v:v + 1],
                                                     seg_ps(6, 7, v), ALU.mult, ALU.mult)
            ins.then_inc(h_tmp, 1)
            if m >= 1:
                rest(m - 1)
        rest(KC - 1)

    def quarter_scratch(t, layer, q, n):
        return t[layer, q].rearrange("p (a t c) -> p a t c", a=2, t=QT, c=n)

    def mix_sync(sp, M, pre):
        l = M.layer
        wi = w_in[l].rearrange("(k p) n -> p k n", p=128)
        wg = w_glu[l].rearrange("(k p) n -> p k n", p=128)
        wo = w_out[l].rearrange("(k p) n -> p k n", p=128)
        units = [wi[:, :, m * 128:(m + 1) * 128] for m in range(8)] + [wg[:, :, j * 256:(j + 1) * 256] for j in range(2)]
        units += [wo[:, :, m * 128:(m + 1) * 128] for m in range(8)]
        for i in range(RAW_SLOTS):
            load_unit(sp, i, 0, M.base, units[i])
        sp.wait_ge(h_lo, KC * pre.nth + KC)
        for i, (bt, ct) in enumerate(((b_re, c_re), (b_im, c_im))):
            sp.dma_start(brow[:, i], bt[l].rearrange("d (q g) p h -> (g p) (d q) h", g=2)).then_inc(rows, 16)
            cv = ct[l].rearrange("d (a b g) h p -> b h (d a) g p", a=2, b=8, g=2)
            for b in range(8):
                for g in range(2):
                    sp.dma_start(crow[b * GH:(b + 1) * GH, i, :, g * NST:(g + 1) * NST], cv[b, :, :, g, :])\
                        .then_inc(rows, 16)
        sp.dma_start(fmixW[:], w_fmix[l].rearrange("n p d -> p n d")).then_inc(rows, 16)
        sp.dma_start(headDft[:], dft_head).then_inc(rows, 16)
        for i in range(RAW_SLOTS, 12):
            load_unit(sp, i, 0, M.base, units[i])
        sp.wait_ge(w_used, M.base + 8)
        sp.dma_start(seqC[:], dft_lat[0]).then_inc(dft, 16)
        sp.dma_start(seqS[:], dft_lat[1]).then_inc(dft, 16)
        sp.dma_start(ctxCS[:], dft_ctx).then_inc(dft, 16)
        sp.wait_ge(gen_store, M.n0["gen_store"] + 16 * 3 * HC)
        sp.wait_ge(e_store, M.n0["e_store"] + 16 * HC)

        def load_set(q):
            s = q % 2
            sp.dma_start(VTs[s][:], quarter_scratch(VT_d, l, q, 128)).then_inc(set_a[s], 16)
            sp.dma_start(Es[s][:], quarter_scratch(E_d, l, q, NCH)).then_inc(set_a[s], 16)
            sp.dma_start(Ws[s][:], quarter_scratch(W_d, l, q, 128)).then_inc(set_c[s], 16)
            sv = strip_d[l, q].rearrange("h (g w) -> h g w", w=STRIP)
            for t in range(T8):
                sp.dma_start(Tz[s][t * GH:(t + 1) * GH, :, :], sv[:, :, (T8 - 1 - t) * GH:(T8 - 1 - t) * GH + 128])\
                    .then_inc(set_c[s], 16)

        def load_chunks(q):
            s = q % 2
            uv = u_d[l, q].rearrange("(g h) (t c) -> t h g c", g=QG, t=T8)
            for t in range(T8):
                sp.dma_start(UC[t * GH:(t + 1) * GH, s, :, :], uv[t]).then_inc(set_a[s], 16)

        load_set(0)
        sp.wait_ge(u_store, M.n0["u_store"] + 16 * HC)
        sp.wait_ge(f_ps, M.n0["f_ps"] + HC)
        load_chunks(0)
        load_set(1)
        load_chunks(1)
        sp.dma_start(UP2[:], u_d[l].rearrange("m p (t c) -> p m t c", t=T8)).then_inc(u_back, 16)
        for q in range(HC):
            if q + 2 < HC:
                sp.wait_ge(y_ps, M.n0["y_ps"] + q + 1)
                sp.wait_ge(states, M.n0["states"] + q + 1)
                load_set(q + 2)
                load_chunks(q + 2)
            sp.wait_ge(y_taken, M.n0["y_taken"] + q + 1)
            yv = y_d[l, q].rearrange("p (g c) -> p g c", g=QG)
            sp.dma_start(yv[:, :, M.c0:NCH], YC[:, :, M.c0:NCH]).then_inc(y_store, 16)
            sp.wait_ge(y_store, M.n0["y_store"] + 16 * (q + 1))
            if q >= 1:
                sp.wait_ge(gelu, M.n0["gelu"] + q)
            yv = y_d[l, q].rearrange("(t h) (g c) -> g h t c", t=T8, g=QG)
            nch = NCH - M.c0
            for g in range(QG):
                sp.dma_start(YP[g * GH:(g + 1) * GH, 0:T8 * nch].rearrange("h (t c) -> h t c", t=T8),
                             yv[g][:, :, M.c0:NCH]).then_inc(y_back, 16)
        for i in range(12, 18):
            load_unit(sp, i, 0, M.base, units[i])

    def mix_pool(pool, M, pre):
        l = M.layer
        pool.wait_ge(h_lo, KC * pre.nth + KC)
        tt = nc.gpsimd.tensor_tensor
        plink(pool, nc.gpsimd.tensor_copy(piv[:, 0, 0, :], P8R[:, l * LD:(l + 1) * LD]))
        plink(pool, nc.gpsimd.tensor_copy(piv[:, 0, 1, :], P8I[:, l * LD:(l + 1) * LD]))
        for i in range(NPIV - 1):
            a, b, na, nb = piv[:, i, 0, :], piv[:, i, 1, :], piv[:, i + 1, 0, :], piv[:, i + 1, 1, :]
            plink(pool, tt(pt[:, 0], a, a, ALU.mult))
            plink(pool, tt(pt[:, 1], b, b, ALU.mult))
            plink(pool, tt(pt[:, 2], pt[:, 0], pt[:, 1], ALU.subtract))
            plink(pool, tt(pt[:, 0], a, b, ALU.mult))
            plink(pool, tt(pt[:, 3], pt[:, 0], pt[:, 0], ALU.add))
            plink(pool, tt(pt[:, 0], pt[:, 2], pt[:, 2], ALU.mult))
            plink(pool, tt(pt[:, 1], pt[:, 3], pt[:, 3], ALU.mult))
            plink(pool, tt(pt[:, 0], pt[:, 0], pt[:, 1], ALU.add))
            plink(pool, nc.gpsimd.tensor_scalar(pt[:, 0], pt[:, 0], -0.5, 1.5, ALU.mult, ALU.add))
            plink(pool, tt(na, pt[:, 2], pt[:, 0], ALU.mult))
            plink(pool, tt(nb, pt[:, 3], pt[:, 0], ALU.mult))
        for q in range(HC):
            if q:
                pool.wait_ge(e_store, M.n0["e_store"] + 16 * q)
            for d in range(2):
                plink(pool, nc.gpsimd.memset(EG[:, 0, d * QP:(d + 1) * QP, 0:1], 1.0))
                plink(pool, nc.gpsimd.memset(EG[:, 1, d * QP:(d + 1) * QP, 0:1], 0.0))
            for i in range(NPIV):
                n = 1 << i
                w = min(n, NCH - n)
                for d in range(2):
                    ts = slice(d * QP, (d + 1) * QP)
                    er, ei = EG[:, 0, ts, 0:w], EG[:, 1, ts, 0:w]
                    pr, pi = (piv[:, i, j, d * NPAIR + q * QP:d * NPAIR + (q + 1) * QP].unsqueeze(2)
                              .broadcast_to([128, QP, w]) for j in range(2))
                    a, b = et[:, 0, ts, 0:w], et[:, 1, ts, 0:w]
                    plink(pool, tt(a, er, pr, ALU.mult))
                    plink(pool, tt(b, ei, pi, ALU.mult))
                    plink(pool, tt(EG[:, 0, ts, n:n + w], a, b, ALU.subtract))
                    plink(pool, tt(a, er, pi, ALU.mult))
                    plink(pool, tt(b, ei, pr, ALU.mult))
                    plink(pool, tt(EG[:, 1, ts, n:n + w], a, b, ALU.add))
            pool.dma_start(quarter_scratch(E_d, l, q, NCH), EG[:]).then_inc(e_store, 16)

    def mix_tensor(pe, M, pre):
        l, tok0 = M.layer, M.tok0
        pe.wait_ge(h_lo, KC * pre.nth + KC)
        pe.wait_ge(rows, M.n0["rows"] + ROWS)
        for i in range(2):
            for a in range(4):
                ins = nc.tensor.transpose(ps[:, 4 + i, a * 128:(a + 1) * 128], crow[:, i, a, :], ident[:])
        ins.then_inc(ct_ps, 1)

        def proj(m):
            if m >= 2:
                pe.wait_ge(proj_read, M.n0["proj_read"] + m - 1)
            pe.wait_ge(w_lo, M.base + m + 1)
            wh, wl = wtile(M.base + m)
            project(tok0 if m >= HC else 0, m % 2, [(wh[:, k, :], wl[:, k, :]) for k in range(KC)], hH, hL)\
                .then_inc(w_used, 1)

        def matrices(q):
            pe.wait_ge(v_made, M.n0["v_made"] + q + 1)
            if q:
                pe.wait_ge(strip_taken, M.n0["strip_taken"] + q)
            else:
                pe.wait_ge(ct, M.n0["ct"] + 1)
            for a in range(2):
                for t in range(QT):
                    bank, col = 4 + 2 * a + t // 4, (t % 4) * 128
                    ins = nc.tensor.transpose(ps[:, bank, col:col + 128], V[:, a, t, :], ident[:])
            ins.then_inc(vt_ps, 1)
            pe.wait_ge(vt, M.n0["vt"] + q + 1)
            pe.wait_ge(w_made, M.n0["w_made"] + q + 1)
            for g2 in range(2):
                rows = slice(g2 * NST, (g2 + 1) * NST)
                for p in range(QP):
                    bank, col = 4 + 2 * g2 + p // 2, (p % 2) * STRIP
                    fwd, bwd = q * QP + p, NPAIR + q * QP + p
                    parts = [(col + T8 * GH, col + STRIP, [(BbR, fwd, W[rows, 0, p, 0:112]), (BbI, fwd, W[rows, 1, p, 0:112])]),
                             (col, col + 112, [(BbR, bwd, W[rows, 0, QP + p, 16:128]), (BbI, bwd, W[rows, 1, QP + p, 16:128])]),
                             (col + 112, col + 128, [(BbR, fwd, CTr[rows, fwd, :]), (BbI, fwd, CTi[rows, fwd, :]),
                                                     (BbR, bwd, CTr[rows, bwd, :]), (BbI, bwd, CTi[rows, bwd, :])])]
                    for c0, c1, terms in parts:
                        for n, (bt, tile, rhs) in enumerate(terms):
                            ins = nc.tensor.matmul(ps[0:GH, bank, c0:c1], bt[rows, tile, :], rhs,
                                                   start=n == 0, stop=n == len(terms) - 1)
            ins.then_inc(tz_ps, 1)

        for q in range(HC):
            proj(2 * q)
            proj(2 * q + 1)
            matrices(q)

        pe.wait_ge(proj_read, M.n0["proj_read"] + 8)
        for n in range(HC):
            for a in range(2):
                col = (n % 2) * 256 + a * 128
                ins = nc.tensor.matmul(ps[:, n // 2, col:col + 128], headDft[:, a, :], fmixW[:, n, :], start=True, stop=True)
        ins.then_inc(cw_ps, 1)
        pe.wait_ge(cw, M.n0["cw"] + 1)
        pe.wait_ge(strip_taken, M.n0["strip_taken"] + HC)
        b0 = tok0 // 128

        def channels(n):
            if n:
                pe.wait_ge(pq, M.n0["pq"] + n)
            for b in range(b0, 6):
                i = b - b0
                ins = nc.tensor.matmul(ps[:, 2 + i // 2, (i % 2) * 256:(i % 2) * 256 + 256],
                                       XF[:, n, b * 128:(b + 1) * 128], CW[:, n].rearrange("p a d -> p (a d)"),
                                       start=True, stop=True)
            ins.then_inc(pq_ps, 1)

        def tokens(n):
            pe.wait_ge(pq, M.n0["pq"] + n + 1)
            if n == 0:
                pe.wait_ge(dft, M.n0["dft"] + 48)
            if n >= 2:
                pe.wait_ge(f_lo, M.n0["f_lo"] + n - 1)
            bl, bc = (5, 6) if n % 2 == 0 else (7, 0)
            for v, bank, w, blocks in ((LAT, bl, SEQ, range(2, 6)), (CTXV, bc, CTX, range(b0, 2))):
                todo = [(b, a) for b in blocks for a in range(2)]
                for k, (b, a) in enumerate(todo):
                    if v == LAT:
                        rhs = (seqC, seqS)[a][:, b - 2, :]
                    else:
                        rhs = ctxCS[:, a, b, :]
                    ins = nc.tensor.matmul(ps[:, bank, 0:w], PQ[:, n % 2, b, a, :], rhs, start=k == 0, stop=k == len(todo) - 1)
            ins.then_inc(f_ps, 1)

        channels(0)
        for n in range(HC):
            if n + 1 < HC:
                channels(n + 1)
            tokens(n)

        def state_inputs(q):
            s = q % 2
            pe.wait_ge(set_a[s], M.n0["set_a"] + SET_A * (q // 2 + 1))
            if q:
                pe.wait_ge(b_read, M.n0["b_read"] + q)
            else:
                pe.wait_ge(f_lo, M.n0["f_lo"] + HC)
            for a in range(2):
                for t in range(QT):
                    for g2 in range(2):
                        rows = slice(g2 * NST, (g2 + 1) * NST)
                        bank, col = 2 * a + t // QP, (t % QP) * NCH
                        ins = nc.tensor.matmul(ps[rows, bank, col:col + NCH], VTs[s][:, a, t, rows],
                                               UC[:, s, 2 * (t % QP) + g2, :], start=True, stop=True)
            ins.then_inc(b_ps, 1)

        def outputs(q):
            s, c0 = q % 2, M.c0
            pe.wait_ge(set_c[s], M.n0["set_c"] + SET_C * (q // 2 + 1))
            pe.wait_ge(states, M.n0["states"] + q + 1)
            if q >= 2:
                pe.wait_ge(y_taken, M.n0["y_taken"] + q - 1)
            for g2 in range(2):
                rows = slice(g2 * NST, (g2 + 1) * NST)
                bank = 4 + 2 * (q % 2) + g2
                for p in range(QP):
                    dst = ps[:, bank, p * NCH + c0:(p + 1) * NCH]
                    nc.tensor.matmul(dst, Tz[s][:, 2 * p + g2, :], UC[:, s, 2 * p + g2, c0:NCH], start=True, stop=False)
                    for d in range(2):
                        t = d * QP + p
                        nc.tensor.matmul(dst, Ws[s][rows, 0, t, :], SR[rows, t, c0:NCH], start=False, stop=False)
                        ins = nc.tensor.matmul(dst, Ws[s][rows, 1, t, :], SI[rows, t, c0:NCH], start=False, stop=d == 1)
            ins.then_inc(y_ps, 1)

        state_inputs(0)
        for q in range(HC):
            if q + 1 < HC:
                state_inputs(q + 1)
            outputs(q)

        pe.wait_ge(g_lo, M.n0["g_lo"] + HC)
        for m in range(HC):
            n = M.base + 8 + m // 2
            pe.wait_ge(w_lo, n + 1)
            wh, wl = wtile(n, 256)
            cols = slice((m % 2) * 128, (m % 2) * 128 + 128)
            ins = project(tok0, m, [(wh[:, k, cols], wl[:, k, cols]) for k in range(HC)], gH, gL, shift=tok0)
            ins.then_inc(w_used if m % 2 else glu_ps, 1)
        pe.wait_ge(cat_lo, M.n0["cat_lo"] + HC)
        for m in range(KC):
            if m >= 4:
                pe.wait_ge(o_read, M.n0["o_read"] + m - 3)
            n = M.base + 10 + m
            pe.wait_ge(w_lo, n + 1)
            wh, wl = wtile(n)
            project(tok0, m % 4, [(wh[:, k, :], wl[:, k, :]) for k in range(KC)], hH, hL).then_inc(w_used, 1)

    def mix_scalar(act, M, pre):
        l, tok0, c0 = M.layer, M.tok0, M.c0
        T = TOK - tok0
        act.wait_ge(ct_ps, M.n0["ct_ps"] + 1)
        nc.scalar.activation(CTr[:].rearrange("p t h -> p (t h)"), ps[:, 4, :], ACT.Copy)
        nc.scalar.activation(CTi[:].rearrange("p t h -> p (t h)"), ps[:, 5, :], ACT.Copy, scale=-1.0)\
            .then_inc(ct, 1)

        def proj(m):
            act.wait_ge(w_used, M.base + m + 1)
            if m < HC:
                half = NCH // 2
                for h in range(2):
                    ins = nc.scalar.activation(UP[:, m, :, h * half:(h + 1) * half].rearrange("p t c -> p c t"),
                                               ps[:, 2 * (m % 2) + h, 0:TOK // 2].rearrange("p (c t) -> p c t", t=T8),
                                               ACT.Copy)
                ins.then_inc(proj_read, 1)
                act.wait_ge(proj_read, M.n0["proj_read"] + m + 1)
                act.dma_start(u_d[l, m].rearrange("p (t c) -> p t c", t=T8), UP[:, m]).then_inc(u_store, 16)
            else:
                nc.scalar.activation(sb_pair(XF[:, m - HC, :], tok0), ps_pair(m % 2, tok0), ACT.Copy)\
                    .then_inc(proj_read, 1)
            split_hi(act, M.base + m + 3)

        for q in range(HC):
            proj(2 * q)
            proj(2 * q + 1)
            act.wait_ge(vt_ps, M.n0["vt_ps"] + q + 1)
            if q:
                act.wait_ge(gen_store, M.n0["gen_store"] + 48 * q)
            nc.scalar.activation(VTm[:].rearrange("p a t c -> p (a t c)"), ps[:, 4:8, :].rearrange("p b c -> p (b c)"),
                                 ACT.Copy).then_inc(vt, 1)
            act.wait_ge(vt, M.n0["vt"] + q + 1)
            act.dma_start(quarter_scratch(VT_d, l, q, 128), VTm[:]).then_inc(gen_store, 16)
            act.wait_ge(w_made, M.n0["w_made"] + q + 1)
            act.dma_start(quarter_scratch(W_d, l, q, 128), W[:]).then_inc(gen_store, 16)
            act.wait_ge(tz_ps, M.n0["tz_ps"] + q + 1)
            for g2 in range(2):
                for a in range(2):
                    g0 = 4 * a + g2
                    ins = nc.scalar.activation(strip[:, g0:g0 + 3:2, :],
                                               ps[0:GH, 4 + 2 * g2 + a, 0:2 * STRIP].rearrange("p (b c) -> p b c", b=2),
                                               ACT.Copy)
            ins.then_inc(strip_taken, 1)
            act.wait_ge(strip_taken, M.n0["strip_taken"] + q + 1)
            act.dma_start(strip_d[l, q].rearrange("p (g c) -> p g c", g=QG), strip[:]).then_inc(gen_store, 16)

        act.wait_ge(cw_ps, M.n0["cw_ps"] + 1)
        nc.scalar.activation(CW[:].rearrange("p n a d -> p (n a d)"), ps[:, 0:2, :].rearrange("p b c -> p (b c)"),
                             ACT.Copy).then_inc(cw, 1)

        def fbanks(n):
            bl, bc = (5, 6) if n % 2 == 0 else (7, 0)
            return {LAT: ps[:, bl, 0:SEQ], CTXV: ps[:, bc, 0:CTX]}

        for n in range(HC):
            act.wait_ge(f_ps, M.n0["f_ps"] + n + 1)
            for t0, t1, v in token_segments(tok0):
                ins = nc.scalar.activation(hH[:, HC + n, t0:t1], fbanks(n)[v], ACT.Copy)
            ins.then_inc(f_hi, 1)

        def take_y(q):
            act.wait_ge(y_ps, M.n0["y_ps"] + q + 1)
            if q:
                act.wait_ge(y_store, M.n0["y_store"] + 16 * q)
            else:
                act.wait_ge(e_store, M.n0["e_store"] + 16 * HC)
            for g2 in range(2):
                ins = nc.scalar.activation(YC[:, g2::2, c0:NCH],
                                           ps[:, 4 + 2 * (q % 2) + g2, 0:QP * NCH]
                                           .rearrange("p (a c) -> p a c", a=QP)[:, :, c0:NCH], ACT.Copy)
            ins.then_inc(y_taken, 1)

        def do_gelu(q):
            act.wait_ge(y_sum, M.n0["y_sum"] + q + 1)
            nc.scalar.activation(G[:, q, 0:T], YP[:, 0:T], ACT.Gelu_apprx_tanh).then_inc(gelu, 1)

        take_y(0)
        for q in range(HC):
            if q + 1 < HC:
                take_y(q + 1)
            do_gelu(q)
        act.wait_ge(gelu, M.n0["gelu"] + HC)
        for m in range(HC):
            nc.scalar.activation(gH[:, m, 0:T], G[:, m, 0:T], ACT.Copy).then_inc(g_hi, 1)

        def gate(m):
            if m % 2 == 0:
                act.wait_ge(glu_ps, M.n0["glu_ps"] + m // 2 + 1)
            else:
                act.wait_ge(w_used, M.base + 9 + m // 2)
            if m >= 2:
                act.wait_ge(gated, M.n0["gated"] + m - 1)
            dst = sg2[:, m % 2, 0:T]
            if not tok0:
                dst = dst.rearrange("p (h w) -> p h w", h=2)
            nc.scalar.activation(dst, ps_pair(m, tok0), ACT.Sigmoid).then_inc(sig, 1)

        def cat(m):
            act.wait_ge(gated, M.n0["gated"] + m + 1)
            nc.scalar.activation(by_chunk(hH, m, tok0), zt[:, m % 2, 0:T].rearrange("p (t c) -> p t c", t=T8), ACT.Copy)\
                .then_inc(cat_hi, 1)
            if m % 2:
                split_hi(act, M.base + 8 + m // 2 + 3)

        gate(0)
        for m in range(HC):
            if m + 1 < HC:
                gate(m + 1)
            cat(m)
        for m in range(KC):
            split_hi(act, M.base + 10 + m + 3)

    def by_chunk(t, m, tok0):
        return t[:, m, tok0:TOK].rearrange("p (c t) -> p t c", t=T8)

    def mix_vector(dve, M, pre):
        l, tok0, c0 = M.layer, M.tok0, M.c0
        T = TOK - tok0
        tt, stt = nc.vector.tensor_tensor, nc.vector.scalar_tensor_tensor
        L0 = l * LD
        dve.wait_ge(rows, M.n0["rows"] + ROWS)
        fr, fi = (x[:, L0:L0 + LD].unsqueeze(2).broadcast_to([128, LD, GH]) for x in (cfR, cfI))
        for a, b, o, op in ((0, 1, BbR, ALU.subtract), (1, 0, BbI, ALU.add)):
            t1, t2 = (gt[:, 1, i * 4:i * 4 + 4, :].rearrange("p a c -> p (a c)").rearrange("p (t h) -> p t h", h=GH)
                      for i in range(2))
            dlink(dve, tt(t1, brow[:, a], fr, ALU.mult))
            dlink(dve, tt(t2, brow[:, b], fi, ALU.mult))
            dsync(dve)
            dlink(dve, tt(o[:], t1, t2, op))
            dsync(dve)
        dve.wait_ge(ct, M.n0["ct"] + 1)

        def four(x, t0):
            return x[:, t0:t0 + QP, :].unsqueeze(2).broadcast_to([128, QP, T8, GH])

        def powers(t, k0, k1, t0):
            v = t[:, k0:k1 + 1, L0 + t0:L0 + t0 + QP] if k1 > k0 else t[:, k0:(k1 - 1 if k1 else None):-1, L0 + t0:L0 + t0 + QP]
            return v.rearrange("p k t -> p t k").unsqueeze(3).broadcast_to([128, QP, T8, GH])

        def tiles(x, a, d):
            return x[:, a, d * QP:(d + 1) * QP, :].rearrange("p t (k h) -> p t k h", h=GH)

        def state_in(q):
            if q:
                dve.wait_ge(vt_ps, M.n0["vt_ps"] + q)
                dve.wait_ge(w_made, M.n0["w_made"] + q)
            for d, (k0, k1) in enumerate(((T8 - 1, 0), (0, T8 - 1))):
                t0 = d * NPAIR + q * QP
                br, bi = four(BbR, t0), four(BbI, t0)
                pr, pi = powers(LkR, k0, k1, t0), powers(LkI, k0, k1, t0)
                for x, y, o, op in ((br, bi, 0, ALU.subtract), (bi, br, 1, ALU.add)):
                    dsync(dve)
                    dlink(dve, tt(tiles(gt, 0, d), x, pr, ALU.mult))
                    dlink(dve, tt(tiles(gt, 1, d), y, pi, ALU.mult))
                    dsync(dve)
                    ins = tt(tiles(V, o, d), tiles(gt, 0, d), tiles(gt, 1, d), op)
                    if d == 1 and o == 1:
                        ins.then_inc(v_made, 1)
                    else:
                        dlink(dve, ins)

        def state_out(q):
            if q:
                dve.wait_ge(gen_store, M.n0["gen_store"] + 48 * q)
                dve.wait_ge(tz_ps, M.n0["tz_ps"] + q)
            dve.wait_ge(v_made, M.n0["v_made"] + q + 1)
            for d, (k0, k1) in enumerate(((1, T8), (T8, 1))):
                t0 = d * NPAIR + q * QP
                cr, ci = four(CTr, t0), four(CTi, t0)
                pr, pi = powers(LkR, k0, k1, t0), powers(LkI, k0, k1, t0)
                for x, y, o, op in ((cr, ci, 0, ALU.add), (ci, cr, 1, ALU.subtract)):
                    dsync(dve)
                    dlink(dve, tt(tiles(gt, 0, d), x, pr, ALU.mult))
                    dlink(dve, tt(tiles(gt, 1, d), y, pi, ALU.mult))
                    dsync(dve)
                    ins = tt(tiles(W, o, d), tiles(gt, 0, d), tiles(gt, 1, d), op)
                    if d == 1 and o == 1:
                        ins.then_inc(w_made, 1)
                    else:
                        dlink(dve, ins)

        for q in range(HC):
            state_in(q)
            split_lo(dve, M.base + 2 * q + 3)
            state_out(q)
            split_lo(dve, M.base + 2 * q + 4)

        dve.wait_ge(u_store, M.n0["u_store"] + 16 * HC)
        nb = 6 - tok0 // 128

        def channels(n):
            dve.wait_ge(pq_ps, M.n0["pq_ps"] + n + 1)
            if n >= 2:
                dve.wait_ge(f_ps, M.n0["f_ps"] + n - 1)
            nc.vector.tensor_copy(PQ[:, n % 2, 6 - nb:6].rearrange("p b a d -> p (b a d)"),
                                  ps[:, 2:2 + nb // 2, :].rearrange("p b c -> p (b c)")).then_inc(pq, 1)

        def fourier_rest(n):
            bl, bc = (5, 6) if n % 2 == 0 else (7, 0)
            dve.wait_ge(f_hi, M.n0["f_hi"] + n + 1)
            for t0, t1, v in token_segments(tok0):
                src = ps[:, bl, 0:SEQ] if v == LAT else ps[:, bc, 0:CTX]
                ins = tt(hL[:, HC + n, t0:t1], src, hH[:, HC + n, t0:t1].bitcast(f32), ALU.subtract)
            ins.then_inc(f_lo, 1)

        channels(0)
        for n in range(HC):
            if n + 1 < HC:
                channels(n + 1)
            fourier_rest(n)

        def rotate(q):
            s = q % 2
            dve.wait_ge(b_ps, M.n0["b_ps"] + q + 1)
            if q:
                dve.wait_ge(states, M.n0["states"] + q)
            if q == 0:
                for x in (SR, SI):
                    nc.vector.memset(x[:, 0:QP, 0:1], 0.0)
                    dlink(dve, nc.vector.memset(x[:, QP:QT, CCH - 1:CCH], 0.0))
            segs = [(0, 0, NCH, slice(0, NCH)), (1, 0, CCH, slice(CCH - 1, None, -1)), (1, CCH, NCH, slice(NCH - 1, CCH - 1, -1))]
            for d, j0, j1, cols in segs:
                src = [ps[:, 2 * a + d, 0:QP * NCH].rearrange("p (t c) -> p t c", c=NCH)[:, :, cols] for a in range(2)]
                ts = slice(d * QP, (d + 1) * QP)
                er, ei = Es[s][:, 0, ts, j0:j1], Es[s][:, 1, ts, j0:j1]
                for o, a, e in ((za, 0, er), (zb, 1, ei), (zc, 1, er), (zd, 0, ei)):
                    ins = tt(o[:, ts, j0:j1], src[a], e, ALU.mult)
                    last = d == 1 and j0 == CCH and o is zd
                    if last:
                        ins.then_inc(b_read, 1)
                    else:
                        dlink(dve, ins)
            dsync(dve)
            dve.wait_ge(b_read, M.n0["b_read"] + q + 1)
            dlink(dve, tt(za[:], za[:], zb[:], ALU.add))
            dlink(dve, tt(zc[:], zc[:], zd[:], ALU.subtract))
            dsync(dve)
            for t in range(QT):
                col = L0 + (t // QP) * NPAIR + q * QP + t % QP
                decay = r8[:, col:col + 1].broadcast_to([128, NCH])
                dlink(dve, nc.vector.tensor_tensor_scan(zb[:, t, :], decay, za[:, t, :], 0.0, ALU.mult, ALU.add))
                dlink(dve, nc.vector.tensor_tensor_scan(zd[:, t, :], decay, zc[:, t, :], 0.0, ALU.mult, ALU.add))
            if q:
                dve.wait_ge(y_ps, M.n0["y_ps"] + q)
            dsync(dve)
            outs = [(0, 0, NCH - 1, slice(1, NCH)), (1, 0, CCH - 1, slice(CCH - 2, None, -1)),
                    (1, CCH - 1, NCH - 1, slice(NCH - 1, CCH - 1, -1))]
            for o, x, y, op in ((SR, zb, zd, ALU.subtract), (SI, zd, zb, ALU.add)):
                dsync(dve)
                dlink(dve, tt(za[:], x[:], Es[s][:, 0], ALU.mult))
                dlink(dve, tt(zc[:], y[:], Es[s][:, 1], ALU.mult))
                dsync(dve)
                for d, j0, j1, cols in outs:
                    ts = slice(d * QP, (d + 1) * QP)
                    ins = tt(o[:, ts, cols], za[:, ts, j0:j1], zc[:, ts, j0:j1], op)
                    if o is SI and d == 1 and j0:
                        ins.then_inc(states, 1)
                    else:
                        dlink(dve, ins)

        def skip(q):
            nch = NCH - c0
            if q == 0:
                dve.wait_ge(u_back, M.n0["u_back"] + 16)
            dve.wait_ge(y_back, M.n0["y_back"] + 16 * QG * (q + 1))
            yp = YP[:, 0:T].rearrange("p (t c) -> p t c", t=T8)
            stt(yp, UP2[:, q, :, c0:NCH], skipD[:, l * HC + q:l * HC + q + 1], yp, ALU.mult, ALU.add)\
                .then_inc(y_sum, 1)

        rotate(0)
        for q in range(HC):
            if q + 1 < HC:
                rotate(q + 1)
            skip(q)

        for m in range(HC):
            dve.wait_ge(g_hi, M.n0["g_hi"] + m + 1)
            tt(gL[:, m, 0:T], G[:, m, 0:T], gH[:, m, 0:T].bitcast(f32), ALU.subtract).then_inc(g_lo, 1)

        def times_gate(m):
            dve.wait_ge(sig, M.n0["sig"] + m + 1)
            if m >= 2:
                dve.wait_ge(cat_hi, M.n0["cat_hi"] + m - 1)
                dve.wait_ge(cat_lo, M.n0["cat_lo"] + m - 1)
            tt(zt[:, m % 2, 0:T], G[:, m, 0:T], sg2[:, m % 2, 0:T], ALU.mult).then_inc(gated, 1)

        def cat_rest(m):
            dve.wait_ge(cat_hi, M.n0["cat_hi"] + m + 1)
            tt(by_chunk(hL, m, tok0), zt[:, m % 2, 0:T].rearrange("p (t c) -> p t c", t=T8),
               by_chunk(hH, m, tok0).bitcast(f32), ALU.subtract).then_inc(cat_lo, 1)
            if m % 2:
                split_lo(dve, M.base + 8 + m // 2 + 3)

        times_gate(0)
        for m in range(HC):
            if m + 1 < HC:
                times_gate(m + 1)
            cat_rest(m)
        for m in range(KC):
            dve.wait_ge(w_used, M.base + 11 + m)
            nc.vector.tensor_copy(sb_pair(yT[:, m, :], tok0), ps_pair(m % 4, tok0)).then_inc(o_read, 1)
            split_lo(dve, M.base + 10 + m + 3)


    def start_sync(sp):
        rows = "l d (q g) p -> (l d q) (g p)"
        sp.dma_start(prow[0:64, 0, :], lam_re.rearrange(rows, g=2)).then_inc(s_par, 16)
        sp.dma_start(prow[64:128, 0, :], lam_im.rearrange(rows, g=2)).then_inc(s_par, 16)
        sp.dma_start(prow[0:96, 1, :], norm_g.rearrange("l i (m p) -> (l i m) p", p=128)).then_inc(s_par, 16)
        for l in range(DEPTH):
            sp.dma_start(prow[0:72, 2 + l, :], b_ada[l].rearrange("(m p) -> m p", p=128)).then_inc(s_par, 16)
        sp.dma_start(prow[0:8, 4, :], c.rearrange("a (m p) -> (a m) p", p=128)).then_inc(s_par, 16)
        sp.dma_start(prow[8:16, 4, :], c_ctx.rearrange("(m p) -> m p", p=128)).then_inc(s_par, 16)
        sp.dma_start(prow[16:24, 4, :], ssm_d.rearrange("l (m p) -> (l m) p", p=128)).then_inc(s_par, 16)
        for h in range(2):
            sp.dma_start(pdt[64 * h:64 * h + 64, 0:2], log_dt.rearrange("l d (q g) -> (l d q) g", g=2)).then_inc(s_par, 16)
        sp.dma_start(posR[:], pos_row).then_inc(s_pos, 16)
        sp.dma_start(posC[:], pos_col).then_inc(s_pos, 16)
        sp.dma_start(xin[:, 0:2, :], ctx_in[0].rearrange("(b p) d -> p b d", p=128)).then_inc(s_xin, 16)
        sp.dma_start(xin[:, 2:6, :], x[0].rearrange("(b p) d -> p b d", p=128)).then_inc(s_xin, 16)

    def start_pool(pool):
        nc.gpsimd.memset(ident[:], 0.0).then_inc(s_id, 1)
        nc.gpsimd.memset(ones[:], 1.0).then_inc(s_id, 1)
        nc.gpsimd.memset(modrow[:], 0.0).then_inc(s_id, 1)
        pool.wait_ge(s_id, 3)
        nc.gpsimd.affine_select(out=ident[:], in_=ident[:], compare_op=ALU.not_equal, fill=1.0, base=0,
                                pattern=[[-1, 128]], channel_multiplier=1).then_inc(s_id, 1)
        nc.gpsimd.memset(ones[:, 1:2], EPS).then_inc(s_id, 1)
        for R in range(8):
            ada_dma(pool, R, 0, 0, R)

    def start_tensor(pe):
        pe.wait_ge(s_id, 5)
        pe.wait_ge(s_par, 16 * 10)
        pe.wait_ge(s_dt, 1)
        nc.tensor.transpose(ps[:, 6, 0:128], prow[:, 0, :], ident[:])
        nc.tensor.transpose(ps[:, 6, 128:256], prow[:, 5, :], ident[:])
        nc.tensor.transpose(ps[:, 6, 256:352], prow[0:96, 1, :], ident[0:96, 0:96])
        nc.tensor.transpose(ps[:, 6, 384:408], prow[0:24, 4, :], ident[0:24, 0:24])
        for l in range(DEPTH):
            ins = nc.tensor.transpose(ps[:, 7, 128 * l:128 * l + 72], prow[0:72, 2 + l, :], ident[0:72, 0:72])
        ins.then_inc(s_parps, 1)
        pe.wait_ge(s_xin, 32)
        for m in range(KC):
            if m >= 2:
                pe.wait_ge(s_xctx, m - 1)
                pe.wait_ge(s_xlat, m - 1)
            for b in range(6):
                bank, col = (2 * (m % 2), b * 128) if b < 2 else (2 * (m % 2) + 1, b * 128 - CTX)
                ins = nc.tensor.transpose(ps[:, bank, col:col + 128], xin[:, b, m * 128:(m + 1) * 128], ident[:])
            ins.then_inc(s_xps, 1)
        pe.wait_ge(s_xctx, KC)
        pe.wait_ge(s_xlat, KC)
        pe.wait_ge(s_silu, 2)
        pe.wait_ge(s_parT, 3)
        pe.wait_ge(s_lam, 1)
        for R in range(8):
            if R >= 4:
                pe.wait_ge(ada_rows, R - 3)
            ada_ride(pe, R, 0, R % 4, 0)
            if R:
                ada_turn(pe, R - 1, 0, 4 + (R - 1) % 4, 128 * ((R - 1) // 4))

    def start_scalar(act):
        act.wait_ge(s_par, 16 * 10)
        nc.scalar.activation(pdt[:, 2:4], pdt[:, 0:2], ACT.Exp).then_inc(s_exp, 1)
        act.wait_ge(s_parps, 1)
        nc.scalar.activation(lamT[:].rearrange("p a c -> p (a c)"), ps[:, 6, 0:256], ACT.Copy).then_inc(s_lam, 1)
        nc.scalar.activation(gT[:], ps[:, 6, 256:352], ACT.Copy).then_inc(s_parT, 1)
        nc.scalar.activation(adaB[:].rearrange("p (l m) -> p l m", l=DEPTH),
                             ps[:, 7, 0:256].rearrange("p (l m) -> p l m", l=DEPTH)[:, :, 0:72], ACT.Copy).then_inc(s_parT, 1)
        nc.scalar.activation(skipD[:], ps[:, 6, 400:408], ACT.Copy).then_inc(s_parT, 1)
        for v in range(2):
            nc.scalar.activation(siluC[:, :, v], ps[:, 6, 384 + 8 * v:392 + 8 * v], ACT.Silu).then_inc(s_silu, 1)
        act.wait_ge(s_lam, 1)
        nc.scalar.activation(lt[:, 0, :], lamT[:, 1, 0:64], ACT.Exp).then_inc(s_trig, 1)
        nc.scalar.activation(r8[:], lamT[:, 1, 0:64], ACT.Exp, scale=float(T8)).then_inc(s_trig, 1)
        act.wait_ge(s_red, 1)
        nc.scalar.activation(lt[:, 3, :], lt[:, 2, :], ACT.Sin).then_inc(s_trig, 1)
        nc.scalar.activation(lt[:, 4, :], lt[:, 2, :], ACT.Sin, scale=0.5).then_inc(s_trig, 1)
        for m in range(KC):
            act.wait_ge(s_xps, m + 1)
            nc.scalar.activation(xT[:, m, 0:CTX], ps[:, 2 * (m % 2), 0:CTX], ACT.Copy).then_inc(s_xctx, 1)
        for n in range(SPLIT_SLOTS):
            split_hi(act, n)
        for R in range(8):
            take_rows(act, R, 0, R % 4, 0)
            if R:
                take_columns(act, R - 1, 0, 4 + (R - 1) % 4, 128 * ((R - 1) // 4))

    def start_vector(dve):
        tt, ts_, stt = nc.vector.tensor_tensor, nc.vector.tensor_scalar, nc.vector.scalar_tensor_tensor
        dve.wait_ge(s_exp, 1)
        tt(prow[:, 5, :].rearrange("p (g s) -> p g s", g=2), prow[:, 0, :].rearrange("p (g s) -> p g s", g=2),
           pdt[:, 2:4].unsqueeze(2).broadcast_to([128, 2, NST]), ALU.mult).then_inc(s_dt, 1)
        dve.wait_ge(s_lam, 1)
        ang = lamT[:, 1, 64:128]

        def d(ins):
            dlink(dve, ins)
            dsync(dve)

        d(ts_(lt[:, 1, :], ang, 1.0 / TWO_PI, MAGIC, ALU.mult, ALU.add))
        d(ts_(lt[:, 1, :], lt[:, 1, :], MAGIC, None, ALU.subtract))
        d(stt(lt[:, 2, :], lt[:, 1, :], -PI_A, ang, ALU.mult, ALU.add))
        d(stt(lt[:, 2, :], lt[:, 1, :], -PI_B, lt[:, 2, :], ALU.mult, ALU.add))
        d(stt(lt[:, 2, :], lt[:, 1, :], -PI_C, lt[:, 2, :], ALU.mult, ALU.add))
        ts_(lt[:, 2, :], lt[:, 2, :], 3.1415925, -3.1415925, ALU.min, ALU.max).then_inc(s_red, 1)
        for m in range(KC):
            dve.wait_ge(s_xps, m + 1)
            if m == 0:
                dve.wait_ge(s_pos, 32)
            rows = SEQ // GRID_W
            if m < 4:
                pos = posR[:, m, :].unsqueeze(2).broadcast_to([128, rows, GRID_W])
            else:
                pos = posC[:, m - 4, :].unsqueeze(1).broadcast_to([128, rows, GRID_W])
            tt(xT[:, m, CTX:TOK].rearrange("p (r c) -> p r c", c=GRID_W),
               ps[:, 2 * (m % 2) + 1, 0:SEQ].rearrange("p (r c) -> p r c", c=GRID_W), pos, ALU.add).then_inc(s_xlat, 1)
        dve.wait_ge(s_trig, 4)
        mag, sn, sh, cs = lt[:, 0, :], lt[:, 3, :], lt[:, 4, :], lt[:, 5, :]
        t0, t1, t2, t3 = (lt[:, 6 + i, :] for i in range(4))
        d(tt(t0, sh, sh, ALU.mult))
        d(ts_(cs, t0, -2.0, 1.0, ALU.mult, ALU.add))
        dlink(dve, nc.vector.memset(LkR[:, 0, :], 1.0))
        dlink(dve, nc.vector.memset(LkI[:, 0, :], 0.0))
        dlink(dve, tt(LkR[:, 1, :], mag, cs, ALU.mult))
        d(tt(LkI[:, 1, :], mag, sn, ALU.mult))

        def product(o_r, o_i, ar, ai, br, bi):
            dlink(dve, tt(t0, ar, br, ALU.mult))
            dlink(dve, tt(t1, ai, bi, ALU.mult))
            dlink(dve, tt(t2, ar, bi, ALU.mult))
            d(tt(t3, ai, br, ALU.mult))
            dlink(dve, tt(o_r, t0, t1, ALU.subtract))
            d(tt(o_i, t2, t3, ALU.add))

        for k in range(2, T8 + 1):
            a, b = (k + 1) // 2, k // 2
            product(LkR[:, k, :], LkI[:, k, :], LkR[:, a, :], LkI[:, a, :], LkR[:, b, :], LkI[:, b, :])
        lr, li = lamT[:, 0, 0:64], lamT[:, 0, 64:128]
        d(ts_(lt[:, 10, :], LkR[:, 1, :], -1.0, None, ALU.add))
        dlink(dve, tt(t0, lr, lr, ALU.mult))
        d(tt(t1, li, li, ALU.mult))
        d(tt(t0, t0, t1, ALU.add))
        d(nc.vector.reciprocal(lt[:, 11, :], t0))
        dlink(dve, ts_(lt[:, 12, :], li, -1.0, None, ALU.mult))
        dsync(dve)
        product(lt[:, 13, :], lt[:, 14, :], lt[:, 10, :], LkI[:, 1, :], lr, lt[:, 12, :])
        dlink(dve, tt(cfR[:], lt[:, 13, :], lt[:, 11, :], ALU.mult))
        dlink(dve, tt(cfI[:], lt[:, 14, :], lt[:, 11, :], ALU.mult))
        product(lt[:, 13, :], lt[:, 14, :], cs, sn, cs, sn)
        product(lt[:, 15, :], lt[:, 16, :], lt[:, 13, :], lt[:, 14, :], lt[:, 13, :], lt[:, 14, :])
        product(lt[:, 13, :], lt[:, 14, :], lt[:, 15, :], lt[:, 16, :], lt[:, 15, :], lt[:, 16, :])
        dlink(dve, tt(t0, lt[:, 13, :], lt[:, 13, :], ALU.mult))
        d(tt(t1, lt[:, 14, :], lt[:, 14, :], ALU.mult))
        d(tt(t0, t0, t1, ALU.add))
        d(ts_(t0, t0, -0.5, 1.5, ALU.mult, ALU.add))
        dlink(dve, tt(P8R[:], lt[:, 13, :], t0, ALU.mult))
        dlink(dve, tt(P8I[:], lt[:, 14, :], t0, ALU.mult))
        dsync(dve)
        for n in range(SPLIT_SLOTS):
            split_lo(dve, n)
        dve.wait_ge(s_parT, 3)
        dve.wait_ge(ada_taken, 7)

    def end_tensor(pe, N):
        pe.wait_ge(x_new, KC * N.nth + KC)
        for b in range(4):
            if b >= 2:
                pe.wait_ge(s_ocp, b - 1)
            for m in range(KC):
                bank = 4 + 2 * (b % 2) + m // 4
                ins = nc.tensor.transpose(ps[:, bank, (m % 4) * 128:(m % 4) * 128 + 128],
                                          xT[:, m, CTX + b * 128:CTX + (b + 1) * 128], ident[:])
            ins.then_inc(s_ops, 1)

    def end_scalar(act, N):
        for b in range(4):
            act.wait_ge(s_ops, b + 1)
            bank = 4 + 2 * (b % 2)
            nc.scalar.activation(ostage[:, b, :], ps[:, bank:bank + 2, :].rearrange("p b c -> p (b c)"), ACT.Copy)\
                .then_inc(s_ocp, 1)

    def end_sync(sp):
        for b in range(4):
            sp.wait_ge(s_ocp, b + 1)
            sp.dma_start(out[0, b * 128:(b + 1) * 128, :], ostage[:, b, :]).then_inc(s_out, 16)
        sp.wait_ge(s_out, 64)
        for M in (M0, M1):
            sp.wait_ge(u_store, M.n0["u_store"] + 16 * HC)
            sp.wait_ge(gen_store, M.n0["gen_store"] + 48 * HC)
            sp.wait_ge(e_store, M.n0["e_store"] + 16 * HC)
            sp.wait_ge(y_store, M.n0["y_store"] + 16 * HC)

    with stack:
        block = stack.enter_context(nc.Block())

        @block.sync
        def _(sp):
            start_sync(sp)
            for (kind, S, _, _), pre in zip(plan, pres):
                (ffn_sync if kind == "ffn" else lambda e, s: mix_sync(e, s, pre))(sp, S)
            end_sync(sp)

        @block.gpsimd
        def _(pool):
            start_pool(pool)
            pool.wait_ge(w_lo, SPLIT_SLOTS)
            add_squares(pool, pres[0], sq_x, sumX, sum_x)
            for (kind, S, N, nxt), pre in zip(plan, pres):
                (ffn_pool if kind == "ffn" else mix_pool)(pool, S, pre)
                add_squares(pool, N, sq_y, sumY, sum_y)
                if nxt:
                    add_squares(pool, nxt, sq_x, sumX, sum_x)

        @block.tensor
        def _(pe):
            start_tensor(pe)
            pre_tensor(pe, pres[0])
            for (kind, S, N, nxt), pre in zip(plan, pres):
                (ffn_tensor if kind == "ffn" else mix_tensor)(pe, S, pre)
                post_tensor(pe, N, S)
                if nxt:
                    pre_tensor(pe, nxt)
            end_tensor(pe, plan[-1][2])

        @block.scalar
        def _(act):
            start_scalar(act)
            act.wait_ge(s_xctx, KC)
            pre_scalar(act, pres[0], s_xlat, 0)
            for (kind, S, N, nxt), pre in zip(plan, pres):
                if kind == "ffn":
                    ffn_scalar(act, S)
                else:
                    mix_scalar(act, S, pre)
                post_scalar(act, N, S)
                if nxt:
                    pre_scalar(act, nxt, x_new, KC * N.nth)
            end_scalar(act, plan[-1][2])

        @block.vector
        def _(dve):
            start_vector(dve)
            pre_vector(dve, pres[0])
            for (kind, S, N, nxt), pre in zip(plan, pres):
                if kind == "ffn":
                    ffn_vector(dve, S)
                else:
                    mix_vector(dve, S, pre)
                post_vector(dve, N)
                if nxt:
                    pre_vector(dve, nxt)


_INS = ['x', 'c', 'ctx', 'c_ctx', 'w_ada', 'b_ada', 'norm_g', 'ffn1_gu', 'ffn1_down', 'ffn2_gu', 'ffn2_down',
        'w_in', 'w_out', 'ssm_lam_re', 'ssm_lam_im', 'ssm_log_dt', 'ssm_b_re', 'ssm_b_im', 'ssm_c_re', 'ssm_c_im',
        'ssm_d', 'w_glu', 'w_fmix']


def shape_tables():
    quarter = D // 4
    omega = (np.float32(1.0) / (np.float32(10000.0) ** (np.arange(quarter, dtype=np.float32) / np.float32(quarter))))
    omega = omega.astype(np.float32)

    def code(n):
        ang = (np.arange(n, dtype=np.float32)[:, None] * omega[None, :]).astype(np.float32)
        enc = np.concatenate([np.sin(ang), np.cos(ang)], axis=-1).astype(np.float32)
        return np.ascontiguousarray(enc.T.reshape(4, 128, n).transpose(1, 0, 2))

    def dft(n):
        a = np.outer(np.arange(n), np.arange(n)) % n * (2 * np.pi / n)
        return np.cos(a) / np.sqrt(n), np.sin(a) / np.sqrt(n)

    def rows(m):
        n = m.shape[0]
        return m.reshape(n // 128, 128, n).transpose(1, 0, 2)

    cl, sl = dft(SEQ)
    cc, sc = dft(CTX)
    ch, sh = dft(128)
    lat = np.stack([rows(cl), rows(-sl)])
    cx = np.stack([rows(cc), rows(-sc)], axis=1)
    hd = np.stack([ch, sh], axis=1)
    return {"pos_row": code(SEQ // GRID_W), "pos_col": code(GRID_W), "dft_lat": lat, "dft_ctx": cx, "dft_head": hd}


def kernel(**inputs):
    import concourse.bacc as bacc
    from concourse.bass_utils import run_bass_kernel_spmd

    nc = bacc.Bacc("TRN2", target_bir_lowering=False, num_devices=1)
    arrays, args = {}, []
    tables = {k: np.ascontiguousarray(v, dtype=np.float32) for k, v in shape_tables().items()}
    for name in _INS + list(tables):
        a = np.ascontiguousarray(inputs[name]) if name in _INS else tables[name]
        arrays[f"in_{name}_dram"] = a
        args.append(nc.dram_tensor(f"in_{name}_dram", a.shape, mybir.dt.from_np(a.dtype), kind="ExternalInput").ap())
    args.append(nc.dram_tensor("out_0_dram", (1, SEQ, D), f32, kind="ExternalOutput").ap())
    build(nc, *args)
    r = run_bass_kernel_spmd(nc, [arrays], core_ids=[0])
    return r.results[0]["out_0_dram"]
```

```python
import math
from contextlib import ExitStack

import numpy as np

import concourse.bass as bass
from concourse import mybir

DEPTH, D, SEQ, CTX = 2, 1024, 512, 256
TOK = SEQ + CTX
FF = 2816
KC = D // 128
FC = FF // 128
NMOD = 9
EPS = 1e-6
GRID_W = 64
DS = 512
HC = DS // 128
GH = 16
NST = 64
T8 = 8
NCH = TOK // T8
CCH = CTX // T8
NPAIR = 16
LD = 2 * NPAIR
QP = NPAIR // HC
QT = 2 * QP
QG = 2 * QP
STRIP = (2 * T8 - 1) * GH
NPIV = 7
RAW_SLOTS, SPLIT_SLOTS = 4, 3
RIDE = 3
TWO_PI = 2 * math.pi
MAGIC = 12582912.0
PI_A, PI_B = 6.28125, 0.0019350051879882812
PI_C = TWO_PI - PI_A - PI_B

f32, f32r = mybir.dt.float32, mybir.dt.float32r
ALU = mybir.AluOpType
ACT = mybir.ActivationFunctionType

LAT, CTXV = 0, 1


def token_segments(tok0):
    return [(CTX, TOK, LAT)] if tok0 else [(0, CTX, CTXV), (CTX, TOK, LAT)]


def build(nc, x, c, ctx_in, c_ctx, w_ada, b_ada, norm_g, ffn1_gu, ffn1_down, ffn2_gu, ffn2_down, w_in, w_out,
          lam_re, lam_im, log_dt, b_re, b_im, c_re, c_im, ssm_d, w_glu, w_fmix,
          pos_row, pos_col, dft_lat, dft_ctx, dft_head, out):
    stack = ExitStack()
    K = 1024
    BASE = 16512

    def sb(name, shape, kb, dt=f32):
        return nc.alloc_sbuf_tensor_at(name, shape, dt, offset=BASE + int(kb * K))

    def sem(name):
        return stack.enter_context(nc.semaphore(name))

    def scratch(name, shape):
        return nc.dram_tensor(name, shape, f32, kind="Internal").ap()

    xT = sb("xT", [128, KC, TOK], 0)
    hH = sb("hH", [128, KC, TOK], 24, f32r)
    hL = sb("hL", [128, KC, TOK], 48, f32r)
    raw = sb("raw", [128, RAW_SLOTS, 1024], 72)
    wH = sb("wH", [128, SPLIT_SLOTS, 1024], 88, f32r)
    wL = sb("wL", [128, SPLIT_SLOTS, 1024], 100, f32r)
    small = [112.0]

    def keep(name, shape):
        t = sb(name, shape, small[0])
        n = int(np.prod(shape[1:])) * 4
        small[0] += ((n + 31) // 32 * 32) / K
        return t

    modraw = keep("modraw", [128, DEPTH * NMOD * KC, 2])
    gT = keep("gT", [128, DEPTH * 6 * KC])
    adaB = keep("adaB", [128, DEPTH * NMOD * KC])
    ident = keep("ident", [128, 128])
    ones = keep("ones", [128, 8])
    siluC = keep("siluC", [128, KC, 2])
    skipD = keep("skipD", [128, DEPTH * HC])
    coefA = keep("coefA", [128, KC, 2])
    coefS = keep("coefS", [128, KC, 2])
    coefP = keep("coefP", [128, KC, 2])
    LkR = keep("LkR", [128, T8 + 1, 2 * LD])
    LkI = keep("LkI", [128, T8 + 1, 2 * LD])
    cfR = keep("cfR", [128, 2 * LD])
    cfI = keep("cfI", [128, 2 * LD])
    P8R = keep("P8R", [128, 2 * LD])
    P8I = keep("P8I", [128, 2 * LD])
    r8 = keep("r8", [128, 2 * LD])
    sumsq = keep("sumsq", [128, 8])
    rstd = keep("rstd", [128, 8])
    assert small[0] <= 122, small[0]
    midH = sb("midH", [128, 4, TOK], 122, f32r)
    midL = sb("midL", [128, 4, TOK], 134, f32r)
    yT = sb("yT", [128, KC, TOK], 146)
    adaW = sb("adaW", [128, 2, KC, RIDE * 128], 170)
    sq = sb("sq", [128, KC, TOK], 170)
    sgate = sb("sgate", [128, 2, TOK], 194)
    midF = sb("midF", [128, 2, TOK], 200)
    tmpN = sb("tmpN", [128, 2, TOK], 200)
    adaP = sb("adaP", [128, RIDE * 128], 206)
    modrow = sb("modrow", [128, 128], 206)
    sumY = sb("sumY", [128, TOK], 194)
    rmsX = sb("rmsX", [128, TOK], 197)
    xin = sb("xin", [128, 6, D], 146)
    sq_first = sb("sq_first", [128, KC, TOK], 146)
    ada_early = [adaW[:, 0], adaW[:, 1]] + [sb(f"ada_early{i}", [128, KC, RIDE * 128], 24 + 12 * i)[:] for i in range(4)]
    ada_early += ada_early[0:2]
    prow = sb("prow", [128, 6, 128], 122)
    pdt = sb("pdt", [128, 4], 125)
    posR = sb("posR", [128, 4, SEQ // GRID_W], 125.25)
    posC = sb("posC", [128, 4, GRID_W], 125.5)
    lamT = sb("lamT", [128, 2, 128], 127)
    cT = sb("cT", [128, 2 * KC + DEPTH * HC], 128.25)
    lt = sb("lt", [128, 20, 2 * LD], 129)
    CTr = sb("CTr", [128, LD, GH], 122)
    CTi = sb("CTi", [128, LD, GH], 124)
    BbR = sb("BbR", [128, LD, GH], 126)
    BbI = sb("BbI", [128, LD, GH], 128)
    crow = sb("crow", [128, 2, 4, 128], 130)
    V = sb("V", [128, 2, QT, 128], 130)
    brow = sb("brow", [128, 2, LD, GH], 138)
    gt = sb("gt", [128, 2, QT, 128], 138)
    W = sb("W", [128, 2, QT, 128], 146)
    fmixW = sb("fmixW", [128, HC, 128], 154)
    headDft = sb("headDft", [128, 2, 128], 156)
    XF = sb("XF", [128, HC, TOK], 158)
    UP = sb("UP", [128, HC, T8, NCH], 170)
    VTm = sb("VTm", [128, 2, QT, 128], 182)
    strip = sb("strip", [16, QG, STRIP], 190)
    EG = sb("EG", [128, 2, QT, NCH], 198)
    et = sb("et", [128, 2, QT, 32], 204)
    pt = sb("pt", [128, 4, LD], 204)
    piv = sb("piv", [128, NPIV, 2, LD], 206)
    seqC = sb("seqC", [128, 4, SEQ], 24)
    ctxCS = sb("ctxCS", [128, 2, 2, CTX], 32)
    seqS = sb("seqS", [128, 4, SEQ], 48)
    CW = sb("CW", [128, HC, 2, 128], 56)
    PQ = sb("PQ", [128, 2, 6, 2, 128], 170)
    UP2 = sb("UP2", [128, HC, T8, NCH], 24)
    G = sb("G", [128, HC, TOK], 48)
    Ws = [sb("Ws0", [128, 2, QT, 128], 122), sb("Ws1", [128, 2, QT, 128], 162)]
    VTs = [sb("VTs0", [128, 2, QT, 128], 130), sb("VTs1", [128, 2, QT, 128], 148)]
    Tz = [sb("Tz0", [128, QG, 128], 138), sb("Tz1", [128, QG, 128], 176)]
    Es = [sb("Es0", [128, 2, QT, NCH], 142), sb("Es1", [128, 2, QT, NCH], 156)]
    UC = [sb(f"UC{q}", [128, QG, NCH], kb) for q, kb in enumerate((204, 170, 173, 57))]
    zp = sb("zp", [128, QT, NCH], 180)
    za, zb, zc, zd = (sb(n, [128, QT, NCH], 183 + 3 * i) for i, n in enumerate(["za", "zb", "zc", "zd"]))
    SR = sb("SR", [128, QT, NCH], 195)
    SI = sb("SI", [128, QT, NCH], 198)
    YC = sb("YC", [128, QG, NCH], 201)
    YP = sb("YP", [128, TOK], 204)
    gH = sb("gH", [128, HC, TOK], 122, f32r)
    gL = sb("gL", [128, HC, TOK], 134, f32r)
    zt = sb("zt", [128, 2, TOK], 180)
    sg2 = sb("sg2", [128, 2, TOK], 186)
    ostage = sb("ostage", [128, 4, D], 24)

    ps = stack.enter_context(nc.psum_tensor("ps", [128, 8, 512], f32))

    W_d = scratch("W_d", [DEPTH, HC, 128, 2 * QT * 128])
    VT_d = scratch("VT_d", [DEPTH, HC, 128, 2 * QT * 128])
    E_d = scratch("E_d", [DEPTH, HC, 128, 2 * QT * NCH])
    strip_d = scratch("strip_d", [DEPTH, HC, 16, QG * STRIP])
    u_d = scratch("u_d", [DEPTH, HC, 128, TOK])
    y_d = scratch("y_d", [DEPTH, HC, 128, QG * NCH])

    raw_ready = [sem(f"raw_ready{i}") for i in range(RAW_SLOTS)]
    w_hi = sem("w_hi")
    w_lo = sem("w_lo")
    w_used = sem("w_used")
    dve_chain, pool_chain = sem("dve_chain"), sem("pool_chain")
    counts = {"dve": 0, "pool": 0}

    def dlink(dve, ins):
        counts["dve"] += 1
        ins.then_inc(dve_chain, 1)

    def dsync(dve):
        dve.wait_ge(dve_chain, counts["dve"])

    def plink(pool, ins):
        counts["pool"] += 1
        ins.then_inc(pool_chain, 1)
        pool.wait_ge(pool_chain, counts["pool"])

    ada_first = [sem(f"ada_first{i}") for i in range(6)]
    ada_ready = [sem("ada_ready0"), sem("ada_ready1")]
    ada_step = sem("ada_step")
    ada_used = sem("ada_used")
    ada_rows = sem("ada_rows")
    ada_turned = sem("ada_turned")
    ada_taken = sem("ada_taken")

    unit = 0

    NPH = FC // 2
    BODIES = (NPH - 1) // 2
    ROWS = 16 * (2 + 2 * 16)
    SET_A = 16 * (2 + T8)
    SET_C = 16 * (1 + T8)
    FFN_COUNTS = {"down_ready": (KC - 1) * NPH, "gate_read": FC, "up_read": FC, "down_read": KC * (NPH + 1),
                  "mid_hi": FC, "mid_lo": FC}
    MIX_COUNTS = {"proj_read": 8, "rows": ROWS, "fmix_in": 32, "ct_ps": 1, "ct": 1, "v_made": HC, "w_made": HC, "vt_ps": HC, "vt": HC,
                  "tz_ps": HC, "strip_taken": HC, "e_store": 16 * HC, "u_store": 16 * HC, "gen_store": 48 * HC, "dft": 48,
                  "cw_ps": 1, "cw": 1, "pq_ps": HC, "pq": HC, "f_ps": HC, "f_hi": HC, "f_lo": HC, "u_back": 16,
                  "b_ps": HC, "b_read": HC, "scanned": HC, "states": HC, "states_im": HC - 1, "y_ps": HC, "y_taken": HC, "y_store": 16 * HC, "y_back": 16 * QG * HC,
                  "y_sum": HC, "gelu": HC, "g_hi": HC, "g_lo": HC, "glu_ps": 2, "sig": HC, "gated": HC, "cat_hi": HC,
                  "cat_lo": HC, "o_read": 8, "set_a": 2 * SET_A, "set_c": 2 * SET_C}
    down_ready = sem("down_ready")
    gate_read = sem("gate_read")
    up_read = sem("up_read")
    down_read = sem("down_read")
    mid_hi = sem("mid_hi")
    mid_lo = sem("mid_lo")
    sq_y = sem("sq_y")
    sum_y, all_y = sem("sum_y"), sem("all_y")
    ss_y = sem("ss_y")
    sd_y = sem("sd_y")
    rs_y = sem("rs_y")
    bc_y = sem("bc_y")
    y_norm = sem("y_norm")
    x_new = sem("x_new")
    x_new_pool = sem("x_new_pool")
    sq_x = sem("sq_x")
    ss_x = sem("ss_x")
    sd_x = sem("sd_x")
    rs_x = sem("rs_x")
    h_tmp = sem("h_tmp")
    h_hi = sem("h_hi")
    h_lo = sem("h_lo")
    proj_read = sem("proj_read")
    rows = sem("rows")
    fmix_in = sem("fmix_in")
    ct_ps = sem("ct_ps")
    ct = sem("ct")
    v_made = sem("v_made")
    w_made = sem("w_made")
    vt_ps = sem("vt_ps")
    vt = sem("vt")
    tz_ps = sem("tz_ps")
    strip_taken = sem("strip_taken")
    e_store = sem("e_store")
    u_store = sem("u_store")
    gen_store = sem("gen_store")
    dft = sem("dft")
    cw_ps = sem("cw_ps")
    cw = sem("cw")
    pq_ps = sem("pq_ps")
    pq = sem("pq")
    f_ps = sem("f_ps")
    f_hi = sem("f_hi")
    f_lo = sem("f_lo")
    u_back = sem("u_back")
    b_ps = sem("b_ps")
    b_read = sem("b_read")
    scanned = sem("scanned")
    states = sem("states")
    states_im = sem("states_im")
    y_ps = sem("y_ps")
    y_taken = sem("y_taken")
    y_store = sem("y_store")
    y_back = sem("y_back")
    y_sum = sem("y_sum")
    gelu = sem("gelu")
    g_hi = sem("g_hi")
    g_lo = sem("g_lo")
    glu_ps = sem("glu_ps")
    sig = sem("sig")
    gated = sem("gated")
    cat_hi = sem("cat_hi")
    cat_lo = sem("cat_lo")
    o_read = sem("o_read")
    set_a = [sem("set_a0"), sem("set_a1")]
    set_c = [sem("set_c0"), sem("set_c1")]
    made = {"ffn": 0, "mix": 0, "post": 0, "pre": 0}

    class Section:

        def __init__(self, kind, totals):
            self.n0 = {n: made[kind] * totals[n] for n in totals}
            self.nth = made[kind]
            made[kind] += 1

    def make_ffn(tag, layer, gu, down, tok0, ride0):
        nonlocal unit
        F = Section("ffn", FFN_COUNTS)
        F.tag, F.layer, F.tok0, F.ride0, F.base = tag, layer, tok0, ride0, unit
        unit += 6 * (FC // 2)
        F.late = [unit + 1, unit + 2]
        F.gu = gu[layer].rearrange("(k p) n -> p k n", p=128)
        F.down = down[layer].rearrange("(f p) n -> p f n", p=128)
        return F

    def make_norm(layer, k, tok0, weight):
        N = Section("post", {})
        N.layer, N.k, N.tok0, N.weight = layer, k, tok0, weight
        return N

    def make_pre(layer, k, tok0):
        N = Section("pre", {})
        N.layer, N.k, N.tok0, N.sq = layer, k, tok0, sq
        return N

    def make_mixer(tag, layer):
        nonlocal unit
        M = Section("mix", MIX_COUNTS)
        M.tag, M.layer, M.base = tag, layer, unit
        unit += 8 + 2 + 8
        M.late = [unit + 2]
        M.tok0 = CTX if layer == DEPTH - 1 else 0
        M.c0 = M.tok0 // T8
        return M

    pre_first = make_pre(0, 0, 0)
    pre_first.sq = sq_first
    F1_0 = make_ffn("f10", 0, ffn1_gu, ffn1_down, 0, 8)
    M0 = make_mixer("m0", 0)
    F2_0 = make_ffn("f20", 0, ffn2_gu, ffn2_down, 0, 28)
    F1_1 = make_ffn("f11", 1, ffn1_gu, ffn1_down, 0, None)
    M1 = make_mixer("m1", 1)
    F2_1 = make_ffn("f21", 1, ffn2_gu, ffn2_down, CTX, None)
    plan = []
    plan.append(("ffn", F1_0, make_norm(0, 0, 0, 0.5), make_pre(0, 1, 0)))
    plan.append(("mix", M0, make_norm(0, 1, 0, 1.0), make_pre(0, 2, 0)))
    plan.append(("ffn", F2_0, make_norm(0, 2, 0, 0.5), make_pre(1, 0, 0)))
    plan.append(("ffn", F1_1, make_norm(1, 0, 0, 0.5), make_pre(1, 1, 0)))
    plan.append(("mix", M1, make_norm(1, 1, CTX, 1.0), make_pre(1, 2, CTX)))
    plan.append(("ffn", F2_1, make_norm(1, 2, CTX, 0.5), None))
    pres = [pre_first] + [p[3] for p in plan[:-1]]
    for p, pre in zip(plan, pres):
        p[1].pre = pre
    NU = unit

    s_par, s_dt, s_xin, s_pos, s_id = sem("s_par"), sem("s_dt"), sem("s_xin"), sem("s_pos"), sem("s_id")
    s_exp, s_lam, s_parps, s_parT, s_silu, s_lamps = (sem("s_exp"), sem("s_lam"), sem("s_parps"), sem("s_parT"),
                                                      sem("s_silu"), sem("s_lamps"))
    s_xps, s_xctx, s_red, s_trig = sem("s_xps"), sem("s_xctx"), sem("s_red"), sem("s_trig")
    s_ops, s_ocp, s_out, s_xlat = sem("s_ops"), sem("s_ocp"), sem("s_out"), sem("s_xlat")

    def seg_ps(bank_ctx, bank_lat, vec):
        return ps[:, bank_lat, 0:SEQ] if vec == LAT else ps[:, bank_ctx, 0:CTX]

    def halves(tok0):
        return [(CTX, SEQ)] if tok0 else [(0, TOK // 2), (TOK // 2, TOK // 2)]

    def ps_pair(slot, tok0):
        return ps[:, 2 * slot, 0:SEQ] if tok0 else ps[:, 2 * slot:2 * slot + 2, 0:TOK // 2]

    def sb_pair(t, tok0):
        return t[:, CTX:TOK] if tok0 else t[:, 0:TOK].rearrange("p (h w) -> p h w", h=2)

    def load_unit(sp, i, r, F_base, src):
        n = F_base + i
        if n >= RAW_SLOTS:
            sp.wait_ge(w_lo, n - RAW_SLOTS + 1 + 12 * r)
        dst = raw[:, n % RAW_SLOTS, :]
        if len(src.shape) == 3:
            dst = dst.rearrange("p (k c) -> p k c", k=src.shape[1])
        sp.dma_start(dst, src).then_inc(raw_ready[n % RAW_SLOTS], 16)

    def split_hi(act, n, r=0):
        if isinstance(r, int) and n + 12 * r >= NU:
            return
        act.wait_ge(raw_ready[n % RAW_SLOTS], 16 * (n // RAW_SLOTS + 1) + 48 * r)
        if n >= SPLIT_SLOTS:
            act.wait_ge(w_used, n - SPLIT_SLOTS + 1 + 12 * r)
        nc.scalar.activation(wH[:, n % SPLIT_SLOTS, :], raw[:, n % RAW_SLOTS, :], ACT.Copy).then_inc(w_hi, 1)

    def split_lo(dve, n, r=0):
        if isinstance(r, int) and n + 12 * r >= NU:
            return
        dve.wait_ge(w_hi, n + 1 + 12 * r)
        nc.vector.tensor_tensor(wL[:, n % SPLIT_SLOTS, :], raw[:, n % RAW_SLOTS, :],
                                wH[:, n % SPLIT_SLOTS, :].bitcast(f32), ALU.subtract).then_inc(w_lo, 1)

    def three(pairs, dst, first, last):
        n = 0
        for wh, wl, xh, xl in pairs:
            for a, b in ((wh, xh), (wh, xl), (wl, xh)):
                ins = nc.tensor.matmul(dst, a, b, start=first and n == 0, stop=last and n == 3 * len(pairs) - 1)
                n += 1
        return ins

    def project(tok0, slot, wpairs, xh, xl, shift=0):
        for i, (t0, w) in enumerate(halves(tok0)):
            t0 -= shift
            ins = three([(a, b, xh[:, k, t0:t0 + w], xl[:, k, t0:t0 + w]) for k, (a, b) in enumerate(wpairs)],
                        ps[:, 2 * slot + i, 0:w], True, True)
        return ins

    def wtile(n, cols=128):
        s = n % SPLIT_SLOTS
        return (wH[:, s, :].rearrange("p (k c) -> p k c", c=cols), wL[:, s, :].rearrange("p (k c) -> p k c", c=cols))

    def first_groups(pe, base, count, pre):
        pe.wait_ge(w_lo, base + count)
        for k in range(KC):
            pe.wait_ge(h_lo, KC * pre.nth + k + 1)
            for u in range(count):
                wh, wl = wtile(base + u)
                for i, (t0, w) in enumerate(halves(pre.tok0)):
                    ins = three([(wh[:, k, :], wl[:, k, :], hH[:, k, t0:t0 + w], hL[:, k, t0:t0 + w])],
                                ps[:, 2 * u + i, 0:w], k == 0, k == KC - 1)
                if k == KC - 1:
                    ins.then_inc(w_used, 1)


    def ffn_sync(sp, F):
        def gate_up(f, i, r):
            load_unit(sp, i, r, F.base, F.gu[:, :, bass.ds(f * 128, 128)])
            load_unit(sp, i + 1, r, F.base, F.gu[:, :, bass.ds(f * 128 + FF, 128)])

        def body(r):
            for q in range(2):
                gate_up(4 * r + 2 * q + 2, 4 + 6 * q, r)
                gate_up(4 * r + 2 * q + 3, 6 + 6 * q, r)
                for j in range(2):
                    load_unit(sp, 8 + 6 * q + j, r, F.base, F.down[:, 4 * r + 2 * q + j, :])

        gate_up(0, 0, 0)
        gate_up(1, 2, 0)
        with sp.Fori(0, BODIES) as r:
            body(r)
        for j in range(2):
            load_unit(sp, 4 + 12 * BODIES + j, 0, F.base, F.down[:, FC - 2 + j, :])

    RIDES = NMOD * KC // RIDE
    FIRST_RIDES = 8
    PER_BODY = 4

    def ada_source(layer, ride_in_layer):
        return w_ada[layer].rearrange("(k p) n -> p k n", p=128)[:, :, bass.ds(ride_in_layer * (RIDE * 128), RIDE * 128)]

    def ada_dma(act, R, r, layer, ride_in_layer):
        act.wait_ge(ada_used, R - 1 + PER_BODY * r)
        act.dma_start(adaW[:, R % 2, :, :], ada_source(layer, ride_in_layer)).then_inc(ada_ready[R % 2], 16)

    STEPS = 2 * KC

    def ada_steps(dve, R, r, first, last):
        before = STEPS * (R - FIRST_RIDES)
        w = adaW[:, R % 2]
        stt, ts_ = nc.vector.scalar_tensor_tensor, nc.vector.tensor_scalar
        for i in range(first, last):
            k, v = i // 2, 1 - i % 2
            needed = before + (i if i < 4 else i - 1)
            if needed or not isinstance(r, int):
                dve.wait_ge(ada_step, needed + PER_BODY * STEPS * r)
            if i == 0:
                dve.wait_ge(ada_ready[R % 2], 16 * ((R - FIRST_RIDES) // 2 + 1) + 32 * r)
                ins = ts_(adaP[:], w[:, 0], siluC[:, 0, 0:1], None, ALU.mult)
            elif i == 1:
                ins = ts_(w[:, 0], w[:, 0], siluC[:, 0, 1:2], None, ALU.mult)
            else:
                at = w[:, 1 - v]
                ins = stt(at, w[:, k], siluC[:, k, v:v + 1], adaP[:] if i == 3 else at, ALU.mult, ALU.add)
            ins.then_inc(ada_step, 1)

    def ada_ride(pe, R, bank, col):
        pe.wait_ge(ada_first[R % 6], 16 * (R // 6 + 1))
        for j in range(RIDE):
            for k in range(KC):
                ins = nc.tensor.matmul(ps[32 * j:32 * j + 2, bank, col:col + 128], siluC[:, k, :],
                                       ada_early[R][:, k, j * 128:(j + 1) * 128], start=k == 0, stop=k == KC - 1)
        ins.then_inc(ada_used, 1)

    def ada_turn(pe, R, bank, col):
        pe.wait_ge(ada_rows, R + 1)
        nc.tensor.transpose(ps[:, bank, col:col + 128], modrow[:], ident[:]).then_inc(ada_turned, 1)

    def take_rows(act, R, bank, col):
        act.wait_ge(ada_used, R + 1)
        if R >= 1:
            act.wait_ge(ada_turned, R)
        else:
            act.wait_ge(s_id, 5)
        for j in range(RIDE):
            ins = nc.scalar.activation(modrow[32 * j:32 * j + 2, :], ps[32 * j:32 * j + 2, bank, col:col + 128], ACT.Copy)
        ins.then_inc(ada_rows, 1)

    def take_turned(act, R, bank, col):
        act.wait_ge(ada_turned, R + 1)
        nc.scalar.activation(modraw[:, R * RIDE:(R + 1) * RIDE, :],
                             ps[:, bank, col:col + 32 * RIDE].rearrange("p (a b) -> p a b", b=32)[:, :, 0:2], ACT.Copy)\
            .then_inc(ada_taken, 1)

    def ada_columns(pe, R, r, bank, col):
        pe.wait_ge(ada_step, STEPS * (R - FIRST_RIDES + 1) + PER_BODY * STEPS * r)
        for j in range(RIDE):
            for v in range(2):
                ins = nc.tensor.matmul(ps[:, bank, col + 2 * j + v:col + 2 * j + v + 1],
                                       adaW[:, R % 2, 1 - v, j * 128:(j + 1) * 128], ones[:, 0:1], start=True, stop=True)
        ins.then_inc(ada_used, 1)

    def take_columns(act, R, r, bank, col):
        act.wait_ge(ada_used, R + 1 + PER_BODY * r)
        nc.scalar.activation(modraw[:, bass.ds(R * RIDE + PER_BODY * RIDE * r, RIDE), :],
                             ps[:, bank, col:col + 2 * RIDE].rearrange("p (a b) -> p a b", b=2), ACT.Copy)\
            .then_inc(ada_taken, 1)

    def ffn_tensor(pe, F, pre):
        def gate_up(i, r, j, later, ride, units=(0, 1)):
            for u in units:
                if later is not None:
                    pe.wait_ge(down_read, F.n0["down_read"] + later + 5 + 2 * j + u + 16 * r)
                    if u == 0:
                        pe.wait_ge(gate_read, F.n0["gate_read"] + later // 4 + j + 1 + 4 * r)
                    else:
                        pe.wait_ge(up_read, F.n0["up_read"] + later // 4 + j + 1 + 4 * r)
                if ride is not None and u == 0:
                    ada_columns(pe, ride, r, 4 * j, TOK // 2)
                n = F.base + i + u
                pe.wait_ge(w_lo, n + 1 + 12 * r)
                wh, wl = wtile(n)
                project(F.tok0, 2 * j + u, [(wh[:, k, :], wl[:, k, :]) for k in range(KC)], hH, hL)\
                    .then_inc(w_used, 1)

        def down(i, r, p, last):
            n = F.base + i
            pe.wait_ge(w_lo, n + 2 + 12 * r)
            pe.wait_ge(mid_lo, F.n0["mid_lo"] + 2 * p + 2 + 4 * r)
            (ah, al), (bh, bl) = wtile(n), wtile(n + 1)
            s0 = (2 * p) % 4
            for m in range(KC):
                if last or m >= 4:
                    pe.wait_ge(down_read, F.n0["down_read"] + 8 * (p + 1) - 3 + m + 16 * r)
                elif m % 2 == 0:
                    pe.wait_ge(gate_read, F.n0["gate_read"] + 2 * (p + 1) + m // 2 + 1 + 4 * r)
                else:
                    pe.wait_ge(up_read, F.n0["up_read"] + 2 * (p + 1) + m // 2 + 1 + 4 * r)
                for h, (t0, w) in enumerate(halves(F.tok0)):
                    ins = three([(ah[:, m, :], al[:, m, :], midH[:, s0, t0:t0 + w], midL[:, s0, t0:t0 + w]),
                                 (bh[:, m, :], bl[:, m, :], midH[:, s0 + 1, t0:t0 + w], midL[:, s0 + 1, t0:t0 + w])],
                                ps[:, 2 * (m % 4) + h, 0:w], True, True)
                if m < KC - 1:
                    ins.then_inc(down_ready, 1)
            ins.then_inc(w_used, 2)

        first_groups(pe, F.base, 3, pre)
        gate_up(2, 0, 1, None, None, (1,))
        with pe.Fori(0, BODIES) as r:
            for q in range(2):
                for j in range(2):
                    gate_up(4 + 6 * q + 2 * j, r, j, 8 * q, None if F.ride0 is None else F.ride0 + 2 * q + j)
                down(8 + 6 * q, r, q, False)
        down(4 + 12 * BODIES, 0, NPH - 1, True)

    def loop(eng, F, body, peeled=0):
        n = BODIES - peeled - 1 if F.base + 6 * NPH == NU else BODIES - peeled
        with eng.Fori(0, n) as r:
            body(r)
        for r in range(n, BODIES):
            body(r)

    def ffn_scalar(act, F, N):
        def next_ride(R, r):
            if isinstance(r, int):
                if R + PER_BODY * r < F.ride0 + PER_BODY * BODIES:
                    ada_dma(act, R + PER_BODY * r, 0, *divmod(R + PER_BODY * r, RIDES))
            else:
                layer, first = divmod(R, RIDES)
                ada_dma(act, R, r, layer, first + PER_BODY * r)

        if F.ride0 is not None:
            act.wait_ge(h_lo, KC * F.pre.nth + KC)
            next_ride(F.ride0, 0)
            next_ride(F.ride0 + 1, 0)

        def gate(i, r, f, ride):
            act.wait_ge(w_used, F.base + i + 1 + 12 * r)
            if ride is not None:
                take_columns(act, ride, r, 4 * (f % 2), TOK // 2)
                next_ride(ride + 2, r)
            if f >= 2:
                act.wait_ge(up_read, F.n0["up_read"] + f - 1 + 4 * r)
            nc.scalar.activation(sb_pair(sgate[:, f % 2, :], F.tok0), ps_pair(2 * (f % 2), F.tok0), ACT.Silu)\
                .then_inc(gate_read, 1)
            split_hi(act, F.base + i + 3, r)

        def up(i, r, f):
            act.wait_ge(up_read, F.n0["up_read"] + f + 1 + 4 * r)
            nc.scalar.activation(midH[:, f % 4, F.tok0:TOK], midF[:, f % 2, F.tok0:TOK], ACT.Copy).then_inc(mid_hi, 1)
            split_hi(act, F.base + i + 3, r)

        for j in range(2):
            gate(2 * j, 0, j, None)
            up(2 * j + 1, 0, j)
        def body(r):
            for q in range(2):
                for j in range(2):
                    i, f = 4 + 6 * q + 2 * j, 2 + 2 * q + j
                    gate(i, r, f, None if F.ride0 is None else F.ride0 + 2 * q + j)
                    up(i + 1, r, f)
                split_hi(act, F.base + 8 + 6 * q + 3, r)
                split_hi(act, F.base + 9 + 6 * q + 3, r)

        loop(act, F, body, 0 if F.ride0 is None else 2)
        for m in range(KC):
            square_y(act, N, F, m)

    def ffn_vector(dve, F):
        for m in range(KC):
            nc.vector.memset(yT[:, m, F.tok0:TOK], 0.0).then_inc(down_read, 1)

        def up(i, r, f):
            dve.wait_ge(w_used, F.base + i + 1 + 12 * r)
            dve.wait_ge(gate_read, F.n0["gate_read"] + f + 1 + 4 * r)
            if f >= 2:
                dve.wait_ge(mid_hi, F.n0["mid_hi"] + f - 1 + 4 * r)
                dve.wait_ge(mid_lo, F.n0["mid_lo"] + f - 1 + 4 * r)
            nc.vector.tensor_tensor(sb_pair(midF[:, f % 2, :], F.tok0), ps_pair(2 * (f % 2) + 1, F.tok0),
                                    sb_pair(sgate[:, f % 2, :], F.tok0), ALU.mult).then_inc(up_read, 1)
            split_lo(dve, F.base + i + 3, r)
            dve.wait_ge(mid_hi, F.n0["mid_hi"] + f + 1 + 4 * r)
            nc.vector.tensor_tensor(midL[:, f % 4, F.tok0:TOK], midF[:, f % 2, F.tok0:TOK],
                                    midH[:, f % 4, F.tok0:TOK].bitcast(f32), ALU.subtract).then_inc(mid_lo, 1)

        def down(i, r, p, ride=None):
            for m in range(KC):
                if ride is not None:
                    ada_steps(dve, ride, r, KC + m, KC + m + 1)
                if m < KC - 1:
                    dve.wait_ge(down_ready, F.n0["down_ready"] + 7 * p + m + 1 + 14 * r)
                else:
                    dve.wait_ge(w_used, F.base + i + 2 + 12 * r)
                dve.wait_ge(down_read, F.n0["down_read"] + 8 * p + m + 1 + 16 * r)
                nc.vector.tensor_tensor(sb_pair(yT[:, m, :], F.tok0), ps_pair(m % 4, F.tok0),
                                        sb_pair(yT[:, m, :], F.tok0), ALU.add).then_inc(down_read, 1)
            if p < NPH - 1:
                split_lo(dve, F.base + i + 3, r)
                split_lo(dve, F.base + i + 4, r)

        for j in range(2):
            if F.ride0 is not None:
                ada_steps(dve, F.ride0, 0, j * KC, (j + 1) * KC)
            split_lo(dve, F.base + 2 * j + 3)
            up(2 * j + 1, 0, j)

        def body(r):
            for q in range(2):
                more = F.ride0 is not None and not (isinstance(r, int) and r == BODIES - 1 and q == 1)
                if F.ride0 is not None:
                    ada_steps(dve, F.ride0 + 2 * q + 1, r, 0, STEPS)
                for j in range(2):
                    i, f = 4 + 6 * q + 2 * j, 2 + 2 * q + j
                    if j and more:
                        ada_steps(dve, F.ride0 + 2 * q + 2, r, 0, KC)
                    split_lo(dve, F.base + i + 3, r)
                    up(i + 1, r, f)
                down(8 + 6 * q, r, q, F.ride0 + 2 * q + 2 if more else None)

        loop(dve, F, body, 0 if F.ride0 is None else 1)
        down(4 + 12 * BODIES, 0, NPH - 1)

    def y_ready(eng, S, m):
        if S.tag.startswith("f"):
            eng.wait_ge(down_read, S.n0["down_read"] + KC * NPH + m + 1)
        else:
            eng.wait_ge(o_read, S.n0["o_read"] + m + 1)

    def add_squares(pool, N):
        for m in range(1, KC - 1):
            pool.wait_ge(sq_y, KC * N.nth + m + 1)
            ins = nc.gpsimd.tensor_tensor(sumY[:, N.tok0:TOK], (sq[:, 0] if m == 1 else sumY)[:, N.tok0:TOK],
                                          sq[:, m, N.tok0:TOK], ALU.add)
            if m < KC - 2:
                plink(pool, ins)
        ins.then_inc(sum_y, 1)

    def add_last_squares(dve, N):
        dve.wait_ge(sum_y, N.nth + 1)
        dve.wait_ge(sq_y, KC * N.nth + KC)
        nc.vector.tensor_tensor(sumY[:, N.tok0:TOK], sumY[:, N.tok0:TOK], sq[:, KC - 1, N.tok0:TOK], ALU.add)\
            .then_inc(all_y, 1)

    POOL_CHUNKS = (1, 3, 5)
    DVE_CHUNKS = tuple(m for m in range(KC) if m not in POOL_CHUNKS)

    def wait_x(eng, N, m):
        if m in POOL_CHUNKS:
            eng.wait_ge(x_new_pool, len(POOL_CHUNKS) * N.nth + POOL_CHUNKS.index(m) + 1)
        else:
            eng.wait_ge(x_new, len(DVE_CHUNKS) * N.nth + DVE_CHUNKS.index(m) + 1)

    def add_to_x(eng, engine, N, m, done):
        engine.tensor_tensor(xT[:, m, N.tok0:TOK], xT[:, m, N.tok0:TOK], tmpN[:, m % 2, N.tok0:TOK], ALU.add)\
            .then_inc(done, 1)

    def post_pool(pool, N):
        for m in POOL_CHUNKS:
            pool.wait_ge(y_norm, KC * N.nth + m + 1)
            add_to_x(pool, nc.gpsimd, N, m, x_new_pool)

    def stat_matmuls(pe, bank, tok0):
        for b in range(tok0 // 128, TOK // 128):
            ins = nc.tensor.matmul(ps[:, bank, b:b + 1], sumY[:, b * 128:(b + 1) * 128], ones[:, 0:1],
                                   start=True, stop=True)
        return ins

    def spread_matmuls(pe, bank_ctx, bank_lat, tok0):
        for b in range(tok0 // 128, TOK // 128):
            bank, col = (bank_ctx, b * 128) if b < 2 else (bank_lat, b * 128 - CTX)
            ins = nc.tensor.matmul(ps[:, bank, col:col + 128], rstd[:, b:b + 1].broadcast_to([128, 128]), ident[:],
                                   start=True, stop=True)
        return ins

    def post_tensor(pe, N, S):
        pe.wait_ge(all_y, N.nth + 1)
        stat_matmuls(pe, 0, N.tok0).then_inc(ss_y, 1)
        pe.wait_ge(rs_y, N.nth + 1)
        spread_matmuls(pe, 2, 3, N.tok0).then_inc(bc_y, 1)

    def pre_tensor(pe, N):
        for m in range(KC):
            pe.wait_ge(sq_x, KC * N.nth + m + 1)
            for t0, t1, v in token_segments(N.tok0):
                ins = nc.tensor.matmul(seg_ps(6, 7, v), ones[:, 0:1].broadcast_to([128, 128]), N.sq[:, m, t0:t1],
                                       start=m == 0, stop=m == KC - 1)
        ins.then_inc(ss_x, 1)

    def root(act, bank, tok0, nth, ready, done):
        b = tok0 // 128
        act.wait_ge(ready, nth + 1)
        nc.scalar.activation(sumsq[:, b:6], ps[:, bank, b:6], ACT.Sqrt, bias=ones[:, 1:2], scale=1.0 / D).then_inc(done, 1)

    def square_y(act, N, S, m):
        y_ready(act, S, m)
        nc.scalar.activation(sq[:, m, N.tok0:TOK], yT[:, m, N.tok0:TOK], ACT.Square).then_inc(sq_y, 1)

    def post_scalar(act, N, S):
        for n in S.late:
            split_hi(act, n)
        root(act, 0, N.tok0, N.nth, ss_y, sd_y)

    def square_x(act, N, wait_chunk):
        for m in range(KC):
            wait_chunk(m)
            nc.scalar.activation(N.sq[:, m, N.tok0:TOK], xT[:, m, N.tok0:TOK], ACT.Square).then_inc(sq_x, 1)

    def pre_scalar(act, N):
        act.wait_ge(ss_x, N.nth + 1)
        for t0, t1, v in token_segments(N.tok0):
            ins = nc.scalar.activation(rmsX[:, t0:t1], seg_ps(6, 7, v), ACT.Sqrt, bias=ones[:, 1:2], scale=1.0 / D)
        ins.then_inc(sd_x, 1)

    def add_shift(act, N):
        for m in range(KC):
            act.wait_ge(h_tmp, KC * N.nth + m + 1)
            for t0, t1, v in token_segments(N.tok0):
                ins = nc.scalar.activation(hH[:, m, t0:t1], tmpN[:, m % 2, t0:t1], ACT.Identity,
                                           bias=coefS[:, m, v:v + 1])
            ins.then_inc(h_hi, 1)

    def mod_chunk(layer, i):
        at = (layer * NMOD + i) * KC
        return modraw[:, at:at + KC, :], adaB[:, at:at + KC].unsqueeze(2).broadcast_to([128, KC, 2])

    def g_chunk(layer, i):
        at = (layer * 6 + i) * KC
        return gT[:, at:at + KC].unsqueeze(2).broadcast_to([128, KC, 2])

    def coef_post(dve, N):
        a, b = mod_chunk(N.layer, 3 * N.k + 2)
        dlink(dve, nc.vector.tensor_tensor(coefP[:], a, b, ALU.add))
        dsync(dve)
        dlink(dve, nc.vector.scalar_tensor_tensor(coefP[:], coefP[:], N.weight, g_chunk(N.layer, 2 * N.k + 1),
                                                  ALU.mult, ALU.mult))

    def coef_pre(dve, N):
        a, b = mod_chunk(N.layer, 3 * N.k + 1)
        dlink(dve, nc.vector.tensor_tensor(coefA[:], a, b, ALU.add))
        dsync(dve)
        dlink(dve, nc.vector.scalar_tensor_tensor(coefA[:], coefA[:], 1.0, g_chunk(N.layer, 2 * N.k), ALU.add, ALU.mult))
        a, b = mod_chunk(N.layer, 3 * N.k)
        dlink(dve, nc.vector.tensor_tensor(coefS[:], a, b, ALU.add))

    def post_vector(dve, N, S):
        coef_post(dve, N)
        add_last_squares(dve, N)
        for n in S.late:
            split_lo(dve, n)
        b = N.tok0 // 128
        dve.wait_ge(sd_y, N.nth + 1)
        nc.vector.reciprocal(rstd[:, b:6], sumsq[:, b:6]).then_inc(rs_y, 1)
        dve.wait_ge(bc_y, N.nth + 1)
        dsync(dve)
        for m in range(KC):
            if m >= 2:
                wait_x(dve, N, m - 2)
            for t0, t1, v in token_segments(N.tok0):
                ins = nc.vector.scalar_tensor_tensor(tmpN[:, m % 2, t0:t1], yT[:, m, t0:t1], coefP[:, m, v:v + 1],
                                                     seg_ps(2, 3, v), ALU.mult, ALU.mult)
            ins.then_inc(y_norm, 1)
            if m in DVE_CHUNKS:
                dve.wait_ge(y_norm, KC * N.nth + m + 1)
                add_to_x(dve, nc.vector, N, m, x_new)

    def inverse_x(dve, N):
        dve.wait_ge(sd_x, N.nth + 1)
        nc.vector.reciprocal(rmsX[:, N.tok0:TOK], rmsX[:, N.tok0:TOK]).then_inc(rs_x, 1)

    def pre_vector(dve, N):
        dve.wait_ge(rs_x, N.nth + 1)
        dsync(dve)

        def rest(m):
            dve.wait_ge(h_hi, KC * N.nth + m + 1)
            for t0, t1, v in token_segments(N.tok0):
                ins = nc.vector.scalar_tensor_tensor(hL[:, m, t0:t1], tmpN[:, m % 2, t0:t1], coefS[:, m, v:v + 1],
                                                     hH[:, m, t0:t1].bitcast(f32), ALU.add, ALU.subtract)
            ins.then_inc(h_lo, 1)

        for m in range(KC):
            if m >= 2:
                dve.wait_ge(h_lo, KC * N.nth + m - 1)
            for t0, t1, v in token_segments(N.tok0):
                ins = nc.vector.scalar_tensor_tensor(tmpN[:, m % 2, t0:t1], xT[:, m, t0:t1], coefA[:, m, v:v + 1],
                                                     rmsX[:, t0:t1], ALU.mult, ALU.mult)
            ins.then_inc(h_tmp, 1)
            if m >= 1:
                rest(m - 1)
        rest(KC - 1)

    def quarter_scratch(t, layer, q, n):
        return t[layer, q].rearrange("p (a t c) -> p a t c", a=2, t=QT, c=n)

    def mix_sync(sp, M, pre):
        l = M.layer
        wi = w_in[l].rearrange("(k p) n -> p k n", p=128)
        wg = w_glu[l].rearrange("(k p) n -> p k n", p=128)
        wo = w_out[l].rearrange("(k p) n -> p k n", p=128)
        units = [wi[:, :, m * 128:(m + 1) * 128] for m in range(8)] + [wg[:, :, j * 256:(j + 1) * 256] for j in range(2)]
        units += [wo[:, :, m * 128:(m + 1) * 128] for m in range(8)]
        for i in range(RAW_SLOTS):
            load_unit(sp, i, 0, M.base, units[i])
        sp.wait_ge(w_used, M.base)
        for i, (bt, ct) in enumerate(((b_re, c_re), (b_im, c_im))):
            sp.dma_start(brow[:, i], bt[l].rearrange("d (q g) p h -> (g p) (d q) h", g=2)).then_inc(rows, 16)
            cv = ct[l].rearrange("d (a b g) h p -> b h (d a) g p", a=2, b=8, g=2)
            for b in range(8):
                for g in range(2):
                    sp.dma_start(crow[b * GH:(b + 1) * GH, i, :, g * NST:(g + 1) * NST], cv[b, :, :, g, :])\
                        .then_inc(rows, 16)
        for i in range(RAW_SLOTS, RAW_SLOTS + 2):
            load_unit(sp, i, 0, M.base, units[i])
        sp.wait_ge(h_lo, KC * pre.nth + KC)
        sp.dma_start(fmixW[:], w_fmix[l].rearrange("n p d -> p n d")).then_inc(fmix_in, 16)
        sp.dma_start(headDft[:], dft_head).then_inc(fmix_in, 16)
        for i in range(RAW_SLOTS + 2, 12):
            load_unit(sp, i, 0, M.base, units[i])
        sp.wait_ge(w_used, M.base + 8)
        sp.dma_start(seqC[:], dft_lat[0]).then_inc(dft, 16)
        sp.dma_start(seqS[:], dft_lat[1]).then_inc(dft, 16)
        sp.dma_start(ctxCS[:], dft_ctx).then_inc(dft, 16)
        sp.wait_ge(gen_store, M.n0["gen_store"] + 16 * 3 * HC)
        sp.wait_ge(u_store, M.n0["u_store"] + 16 * HC)
        sp.wait_ge(e_store, M.n0["e_store"] + 16 * HC)

        def load_states(q):
            sp.dma_start(VTs[q % 2][:], quarter_scratch(VT_d, l, q, 128)).then_inc(set_a[q % 2], 16)

        def load_phases(q):
            sp.dma_start(Es[q % 2][:], quarter_scratch(E_d, l, q, NCH)).then_inc(set_a[q % 2], 16)

        def load_chunks(q):
            uv = u_d[l, q].rearrange("(g h) (t c) -> t h g c", g=QG, t=T8)
            for t in range(T8):
                sp.dma_start(UC[q][t * GH:(t + 1) * GH, :, :], uv[t]).then_inc(set_a[q % 2], 16)

        def load_w(q):
            sp.dma_start(Ws[q % 2][:], quarter_scratch(W_d, l, q, 128)).then_inc(set_c[q % 2], 16)

        def load_toeplitz(q):
            sv = strip_d[l, q].rearrange("h (g w) -> h g w", w=STRIP)
            for t in range(T8):
                sp.dma_start(Tz[q % 2][t * GH:(t + 1) * GH, :, :], sv[:, :, (T8 - 1 - t) * GH:(T8 - 1 - t) * GH + 128])\
                    .then_inc(set_c[q % 2], 16)

        load_chunks(0)
        load_states(0)
        load_phases(0)
        load_w(0)
        load_toeplitz(0)
        sp.wait_ge(f_ps, M.n0["f_ps"] + HC - 1)
        load_chunks(1)
        load_states(1)
        load_chunks(2)
        load_states(2)
        sp.wait_ge(pq, M.n0["pq"] + HC)
        load_phases(1)
        load_w(1)
        sp.wait_ge(f_ps, M.n0["f_ps"] + HC)
        load_toeplitz(1)
        sp.wait_ge(states, M.n0["states"] + 1)
        load_phases(2)
        sp.dma_start(UP2[:], u_d[l].rearrange("m p (t c) -> p m t c", t=T8)).then_inc(u_back, 16)
        sp.wait_ge(b_ps, M.n0["b_ps"] + 2)
        load_states(3)
        load_chunks(3)
        sp.wait_ge(y_ps, M.n0["y_ps"] + 1)
        load_w(2)
        load_toeplitz(2)
        sp.wait_ge(states, M.n0["states"] + 2)
        sp.wait_ge(states_im, M.n0["states_im"] + 1)
        load_phases(3)
        sp.wait_ge(y_ps, M.n0["y_ps"] + 2)
        load_w(3)
        load_toeplitz(3)
        sp.wait_ge(y_ps, M.n0["y_ps"] + HC)
        for i in range(12, 18):
            load_unit(sp, i, 0, M.base, units[i])

    STATE_SEGS = ((0, 0, NCH - 1, slice(1, NCH)), (1, 0, CCH - 1, slice(CCH - 2, None, -1)),
                  (1, CCH - 1, NCH - 1, slice(NCH - 1, CCH - 1, -1)))

    def states_of(M, q):
        if q % 2 == 0:
            return SR, SI
        return [raw[:, (M.base + i) % RAW_SLOTS, 0:QT * NCH].rearrange("p (t c) -> p t c", c=NCH) for i in (12, 13)]

    def state_bank(q):
        return 0 if q else 1

    def mix_pool(pool, M, pre):
        l = M.layer
        pool.wait_ge(h_lo, KC * pre.nth + KC)
        tt = nc.gpsimd.tensor_tensor
        plink(pool, nc.gpsimd.tensor_copy(piv[:, 0, 0, :], P8R[:, l * LD:(l + 1) * LD]))
        plink(pool, nc.gpsimd.tensor_copy(piv[:, 0, 1, :], P8I[:, l * LD:(l + 1) * LD]))
        for i in range(NPIV - 1):
            a, b, na, nb = piv[:, i, 0, :], piv[:, i, 1, :], piv[:, i + 1, 0, :], piv[:, i + 1, 1, :]
            plink(pool, tt(pt[:, 0], a, a, ALU.mult))
            plink(pool, tt(pt[:, 1], b, b, ALU.mult))
            plink(pool, tt(pt[:, 2], pt[:, 0], pt[:, 1], ALU.subtract))
            plink(pool, tt(pt[:, 0], a, b, ALU.mult))
            plink(pool, tt(pt[:, 3], pt[:, 0], pt[:, 0], ALU.add))
            plink(pool, tt(pt[:, 0], pt[:, 2], pt[:, 2], ALU.mult))
            plink(pool, tt(pt[:, 1], pt[:, 3], pt[:, 3], ALU.mult))
            plink(pool, tt(pt[:, 0], pt[:, 0], pt[:, 1], ALU.add))
            plink(pool, nc.gpsimd.tensor_scalar(pt[:, 0], pt[:, 0], -0.5, 1.5, ALU.mult, ALU.add))
            plink(pool, tt(na, pt[:, 2], pt[:, 0], ALU.mult))
            plink(pool, tt(nb, pt[:, 3], pt[:, 0], ALU.mult))
        for q in range(HC):
            if q:
                pool.wait_ge(e_store, M.n0["e_store"] + 16 * q)
            plink(pool, nc.gpsimd.memset(EG[:, 0, :, 0:1], 1.0))
            plink(pool, nc.gpsimd.memset(EG[:, 1, :, 0:1], 0.0))
            for i in range(NPIV):
                n = 1 << i
                w = min(n, NCH - n)

                def both(x):
                    return x.rearrange("p (d t) c -> p d t c", d=2)

                er, ei = both(EG[:, 0, :, 0:w]), both(EG[:, 1, :, 0:w])
                pr, pi = (piv[:, i, j, :].rearrange("p (d g) -> p d g", d=2)[:, :, q * QP:(q + 1) * QP].unsqueeze(3)
                          .broadcast_to([128, 2, QP, w]) for j in range(2))
                a, b = both(et[:, 0, :, 0:w]), both(et[:, 1, :, 0:w])
                plink(pool, tt(a, er, pr, ALU.mult))
                plink(pool, tt(b, ei, pi, ALU.mult))
                plink(pool, tt(both(EG[:, 0, :, n:n + w]), a, b, ALU.subtract))
                plink(pool, tt(a, er, pi, ALU.mult))
                plink(pool, tt(b, ei, pr, ALU.mult))
                plink(pool, tt(both(EG[:, 1, :, n:n + w]), a, b, ALU.add))
            pool.dma_start(quarter_scratch(E_d, l, q, NCH), EG[:]).then_inc(e_store, 16)

        for q in range(1, HC):
            pool.wait_ge(scanned, M.n0["scanned"] + q + 1)
            if q >= 2:
                pool.wait_ge(y_ps, M.n0["y_ps"] + q - 1)
            e = Es[q % 2]
            im = states_of(M, q)[1]
            for d, j0, j1, cols in STATE_SEGS:
                ts = slice(d * QP, (d + 1) * QP)
                plink(pool, tt(im[:, ts, cols], zd[:, ts, j0:j1], e[:, 0, ts, j0:j1], ALU.mult))
            plink(pool, tt(zp[:], zb[:], e[:, 1], ALU.mult))
            for d, j0, j1, cols in STATE_SEGS:
                ts = slice(d * QP, (d + 1) * QP)
                ins = tt(im[:, ts, cols], im[:, ts, cols], zp[:, ts, j0:j1], ALU.add)
                if d == 1 and j0:
                    ins.then_inc(states_im, 1)
                else:
                    plink(pool, ins)

    def mix_tensor(pe, M, pre):
        l, tok0 = M.layer, M.tok0
        pe.wait_ge(rows, M.n0["rows"] + ROWS)
        for i in range(2):
            for a in range(4):
                ins = nc.tensor.transpose(ps[:, 4 + i, a * 128:(a + 1) * 128], crow[:, i, a, :], ident[:])
        ins.then_inc(ct_ps, 1)
        first_groups(pe, M.base, 2, pre)

        def proj(m):
            pe.wait_ge(proj_read, M.n0["proj_read"] + m - 1)
            pe.wait_ge(w_lo, M.base + m + 1)
            wh, wl = wtile(M.base + m)
            project(tok0 if m >= HC else 0, m % 2, [(wh[:, k, :], wl[:, k, :]) for k in range(KC)], hH, hL)\
                .then_inc(w_used, 1)

        def matrices(q):
            pe.wait_ge(v_made, M.n0["v_made"] + q + 1)
            if q:
                pe.wait_ge(strip_taken, M.n0["strip_taken"] + q)
            else:
                pe.wait_ge(ct, M.n0["ct"] + 1)
            for a in range(2):
                for t in range(QT):
                    bank, col = 4 + 2 * a + t // 4, (t % 4) * 128
                    ins = nc.tensor.transpose(ps[:, bank, col:col + 128], V[:, a, t, :], ident[:])
            ins.then_inc(vt_ps, 1)
            pe.wait_ge(vt, M.n0["vt"] + q + 1)
            pe.wait_ge(w_made, M.n0["w_made"] + q + 1)
            for g2 in range(2):
                rows = slice(g2 * NST, (g2 + 1) * NST)
                for p in range(QP):
                    bank, col = 4 + 2 * g2 + p // 2, (p % 2) * STRIP
                    fwd, bwd = q * QP + p, NPAIR + q * QP + p
                    parts = [(col + T8 * GH, col + STRIP, [(BbR, fwd, W[rows, 0, p, 0:112]), (BbI, fwd, W[rows, 1, p, 0:112])]),
                             (col, col + 112, [(BbR, bwd, W[rows, 0, QP + p, 16:128]), (BbI, bwd, W[rows, 1, QP + p, 16:128])]),
                             (col + 112, col + 128, [(BbR, fwd, CTr[rows, fwd, :]), (BbI, fwd, CTi[rows, fwd, :]),
                                                     (BbR, bwd, CTr[rows, bwd, :]), (BbI, bwd, CTi[rows, bwd, :])])]
                    for c0, c1, terms in parts:
                        for n, (bt, tile, rhs) in enumerate(terms):
                            ins = nc.tensor.matmul(ps[0:GH, bank, c0:c1], bt[rows, tile, :], rhs,
                                                   start=n == 0, stop=n == len(terms) - 1)
            ins.then_inc(tz_ps, 1)

        for q in range(HC):
            if q:
                proj(2 * q)
                proj(2 * q + 1)
            matrices(q)

        pe.wait_ge(proj_read, M.n0["proj_read"] + 8)
        pe.wait_ge(fmix_in, M.n0["fmix_in"] + 32)
        for n in range(HC):
            for a in range(2):
                col = (n % 2) * 256 + a * 128
                ins = nc.tensor.matmul(ps[:, n // 2, col:col + 128], headDft[:, a, :], fmixW[:, n, :], start=True, stop=True)
        ins.then_inc(cw_ps, 1)
        pe.wait_ge(cw, M.n0["cw"] + 1)
        pe.wait_ge(strip_taken, M.n0["strip_taken"] + HC)
        b0 = tok0 // 128

        def channels(n):
            if n:
                pe.wait_ge(pq, M.n0["pq"] + n)
            for b in range(b0, 6):
                i = b - b0
                ins = nc.tensor.matmul(ps[:, 2 + i // 2, (i % 2) * 256:(i % 2) * 256 + 256],
                                       XF[:, n, b * 128:(b + 1) * 128], CW[:, n].rearrange("p a d -> p (a d)"),
                                       start=True, stop=True)
            ins.then_inc(pq_ps, 1)

        def tokens(n):
            pe.wait_ge(pq, M.n0["pq"] + n + 1)
            if n == 0:
                pe.wait_ge(dft, M.n0["dft"] + 48)
            if n >= 2:
                pe.wait_ge(f_lo, M.n0["f_lo"] + n - 1)
            bl, bc = (5, 6) if n % 2 == 0 else (7, 0)
            for v, bank, w, blocks in ((LAT, bl, SEQ, range(2, 6)), (CTXV, bc, CTX, range(b0, 2))):
                todo = [(b, a) for b in blocks for a in range(2)]
                for k, (b, a) in enumerate(todo):
                    if v == LAT:
                        rhs = (seqC, seqS)[a][:, b - 2, :]
                    else:
                        rhs = ctxCS[:, a, b, :]
                    ins = nc.tensor.matmul(ps[:, bank, 0:w], PQ[:, n % 2, b, a, :], rhs, start=k == 0, stop=k == len(todo) - 1)
            ins.then_inc(f_ps, 1)

        def state_inputs(q):
            s = q % 2
            pe.wait_ge(set_a[s], M.n0["set_a"] + SET_A * (q // 2 + 1))
            if q:
                pe.wait_ge(b_read, M.n0["b_read"] + q)
            if q == 1:
                pe.wait_ge(f_lo, M.n0["f_lo"] + HC)
            for a in range(2):
                for t in range(QT):
                    for g2 in range(2):
                        rows = slice(g2 * NST, (g2 + 1) * NST)
                        bank, col = state_bank(q) + 2 * a + t // QP, (t % QP) * NCH
                        ins = nc.tensor.matmul(ps[rows, bank, col:col + NCH], VTs[s][:, a, t, rows],
                                               UC[q][:, 2 * (t % QP) + g2, :], start=True, stop=True)
            ins.then_inc(b_ps, 1)

        def outputs(q):
            s, c0 = q % 2, M.c0
            re, im = states_of(M, q)
            pe.wait_ge(set_c[s], M.n0["set_c"] + SET_C * (q // 2 + 1))
            pe.wait_ge(states, M.n0["states"] + q + 1)
            if q:
                pe.wait_ge(states_im, M.n0["states_im"] + q)
            if q >= 2:
                pe.wait_ge(y_taken, M.n0["y_taken"] + q - 1)
            for g2 in range(2):
                rows = slice(g2 * NST, (g2 + 1) * NST)
                bank = 4 + 2 * (q % 2) + g2
                for p in range(QP):
                    dst = ps[:, bank, p * NCH + c0:(p + 1) * NCH]
                    nc.tensor.matmul(dst, Tz[s][:, 2 * p + g2, :], UC[q][:, 2 * p + g2, c0:NCH], start=True, stop=False)
                    for d in range(2):
                        t = d * QP + p
                        nc.tensor.matmul(dst, Ws[s][rows, 0, t, :], re[rows, t, c0:NCH], start=False, stop=False)
                        ins = nc.tensor.matmul(dst, Ws[s][rows, 1, t, :], im[rows, t, c0:NCH], start=False, stop=d == 1)
            ins.then_inc(y_ps, 1)

        channels(0)
        channels(1)
        tokens(0)
        channels(2)
        tokens(1)
        pe.wait_ge(pq, M.n0["pq"] + 3)
        state_inputs(0)
        tokens(2)
        pe.wait_ge(b_read, M.n0["b_read"] + 1)
        channels(3)
        tokens(3)
        for q in range(HC):
            if q + 1 < HC:
                state_inputs(q + 1)
            outputs(q)

        pe.wait_ge(w_lo, M.base + 10)
        for k in range(HC):
            pe.wait_ge(g_lo, M.n0["g_lo"] + k + 1)
            for m in range(HC):
                if k == 0 and m == HC - 1:
                    pe.wait_ge(y_taken, M.n0["y_taken"] + HC)
                wh, wl = wtile(M.base + 8 + m // 2, 256)
                cols = slice((m % 2) * 128, (m % 2) * 128 + 128)
                for i, (t0, w) in enumerate(halves(tok0)):
                    t0 -= tok0
                    ins = three([(wh[:, k, cols], wl[:, k, cols], gH[:, k, t0:t0 + w], gL[:, k, t0:t0 + w])],
                                ps[:, 2 * m + i, 0:w], k == 0, k == HC - 1)
                if k == HC - 1:
                    ins.then_inc(w_used if m % 2 else glu_ps, 1)
        pe.wait_ge(cat_lo, M.n0["cat_lo"] + HC)
        for m in range(KC):
            if m >= 4:
                pe.wait_ge(o_read, M.n0["o_read"] + m - 3)
            n = M.base + 10 + m
            pe.wait_ge(w_lo, n + 1)
            wh, wl = wtile(n)
            project(tok0, m % 4, [(wh[:, k, :], wl[:, k, :]) for k in range(KC)], hH, hL).then_inc(w_used, 1)

    def mix_scalar(act, M, N):
        l, tok0, c0 = M.layer, M.tok0, M.c0
        T = TOK - tok0
        act.wait_ge(ct_ps, M.n0["ct_ps"] + 1)
        nc.scalar.activation(CTr[:].rearrange("p t h -> p (t h)"), ps[:, 4, :], ACT.Copy)
        nc.scalar.activation(CTi[:].rearrange("p t h -> p (t h)"), ps[:, 5, :], ACT.Copy, scale=-1.0)\
            .then_inc(ct, 1)

        def proj(m):
            act.wait_ge(w_used, M.base + m + 1)
            if m < HC:
                half = NCH // 2
                for h in range(2):
                    ins = nc.scalar.activation(UP[:, m, :, h * half:(h + 1) * half].rearrange("p t c -> p c t"),
                                               ps[:, 2 * (m % 2) + h, 0:TOK // 2].rearrange("p (c t) -> p c t", t=T8),
                                               ACT.Copy)
                ins.then_inc(proj_read, 1)
                act.wait_ge(proj_read, M.n0["proj_read"] + m + 1)
                act.dma_start(u_d[l, m].rearrange("p (t c) -> p t c", t=T8), UP[:, m]).then_inc(u_store, 16)
            else:
                nc.scalar.activation(sb_pair(XF[:, m - HC, :], tok0), ps_pair(m % 2, tok0), ACT.Copy)\
                    .then_inc(proj_read, 1)
            split_hi(act, M.base + m + 3)

        for q in range(HC):
            proj(2 * q)
            proj(2 * q + 1)
            act.wait_ge(vt_ps, M.n0["vt_ps"] + q + 1)
            if q:
                act.wait_ge(gen_store, M.n0["gen_store"] + 48 * q)
            nc.scalar.activation(VTm[:].rearrange("p a t c -> p (a t c)"), ps[:, 4:8, :].rearrange("p b c -> p (b c)"),
                                 ACT.Copy).then_inc(vt, 1)
            act.wait_ge(vt, M.n0["vt"] + q + 1)
            act.dma_start(quarter_scratch(VT_d, l, q, 128), VTm[:]).then_inc(gen_store, 16)
            act.wait_ge(w_made, M.n0["w_made"] + q + 1)
            act.dma_start(quarter_scratch(W_d, l, q, 128), W[:]).then_inc(gen_store, 16)
            act.wait_ge(tz_ps, M.n0["tz_ps"] + q + 1)
            for g2 in range(2):
                for a in range(2):
                    g0 = 4 * a + g2
                    ins = nc.scalar.activation(strip[:, g0:g0 + 3:2, :],
                                               ps[0:GH, 4 + 2 * g2 + a, 0:2 * STRIP].rearrange("p (b c) -> p b c", b=2),
                                               ACT.Copy)
            ins.then_inc(strip_taken, 1)
            act.wait_ge(strip_taken, M.n0["strip_taken"] + q + 1)
            act.dma_start(strip_d[l, q].rearrange("p (g c) -> p g c", g=QG), strip[:]).then_inc(gen_store, 16)

        act.wait_ge(cw_ps, M.n0["cw_ps"] + 1)
        nc.scalar.activation(CW[:].rearrange("p n a d -> p (n a d)"), ps[:, 0:2, :].rearrange("p b c -> p (b c)"),
                             ACT.Copy).then_inc(cw, 1)

        def fbanks(n):
            bl, bc = (5, 6) if n % 2 == 0 else (7, 0)
            return {LAT: ps[:, bl, 0:SEQ], CTXV: ps[:, bc, 0:CTX]}

        for n in range(HC):
            act.wait_ge(f_ps, M.n0["f_ps"] + n + 1)
            for t0, t1, v in token_segments(tok0):
                ins = nc.scalar.activation(hH[:, HC + n, t0:t1], fbanks(n)[v], ACT.Copy)
            ins.then_inc(f_hi, 1)

        def take_y(q):
            act.wait_ge(y_ps, M.n0["y_ps"] + q + 1)
            if q:
                act.wait_ge(y_store, M.n0["y_store"] + 16 * q)
            for g2 in range(2):
                ins = nc.scalar.activation(YC[:, g2::2, c0:NCH],
                                           ps[:, 4 + 2 * (q % 2) + g2, 0:QP * NCH]
                                           .rearrange("p (a c) -> p a c", a=QP)[:, :, c0:NCH], ACT.Copy)
            ins.then_inc(y_taken, 1)
            act.wait_ge(y_taken, M.n0["y_taken"] + q + 1)
            act.dma_start(y_d[l, q].rearrange("p (g c) -> p g c", g=QG)[:, :, c0:NCH], YC[:, :, c0:NCH])\
                .then_inc(y_store, 16)
            act.wait_ge(y_store, M.n0["y_store"] + 16 * (q + 1))
            if q:
                act.wait_ge(gelu, M.n0["gelu"] + q)
            yv = y_d[l, q].rearrange("(t h) (g c) -> g h t c", t=T8, g=QG)
            for g in range(QG):
                act.dma_start(YP[g * GH:(g + 1) * GH, 0:T].rearrange("h (t c) -> h t c", t=T8),
                              yv[g][:, :, c0:NCH]).then_inc(y_back, 16)

        def do_gelu(q):
            act.wait_ge(y_sum, M.n0["y_sum"] + q + 1)
            nc.scalar.activation(G[:, q, 0:T], YP[:, 0:T], ACT.Gelu_apprx_tanh).then_inc(gelu, 1)

        def round_g(q):
            act.wait_ge(gelu, M.n0["gelu"] + q + 1)
            nc.scalar.activation(gH[:, q, 0:T], G[:, q, 0:T], ACT.Copy).then_inc(g_hi, 1)

        for q in range(HC):
            take_y(q)
            do_gelu(q)
            if q == HC - 2:
                for i in range(HC - 1):
                    round_g(i)
        round_g(HC - 1)

        def gate(m):
            if m % 2 == 0:
                act.wait_ge(glu_ps, M.n0["glu_ps"] + m // 2 + 1)
            else:
                act.wait_ge(w_used, M.base + 9 + m // 2)
            if m >= 2:
                act.wait_ge(gated, M.n0["gated"] + m - 1)
            dst = sg2[:, m % 2, 0:T]
            if not tok0:
                dst = dst.rearrange("p (h w) -> p h w", h=2)
            nc.scalar.activation(dst, ps_pair(m, tok0), ACT.Sigmoid).then_inc(sig, 1)

        def cat(m):
            act.wait_ge(gated, M.n0["gated"] + m + 1)
            nc.scalar.activation(by_chunk(hH, m, tok0), zt[:, m % 2, 0:T].rearrange("p (t c) -> p t c", t=T8), ACT.Copy)\
                .then_inc(cat_hi, 1)
            if m % 2:
                split_hi(act, M.base + 8 + m // 2 + 3)

        gate(0)
        for m in range(HC):
            if m + 1 < HC:
                gate(m + 1)
            cat(m)
        for m in range(KC):
            if m < KC - 1:
                split_hi(act, M.base + 10 + m + 3)
            square_y(act, N, M, m)

    def by_chunk(t, m, tok0):
        return t[:, m, tok0:TOK].rearrange("p (c t) -> p t c", t=T8)

    def mix_vector(dve, M, pre):
        l, tok0, c0 = M.layer, M.tok0, M.c0
        T = TOK - tok0
        tt, stt = nc.vector.tensor_tensor, nc.vector.scalar_tensor_tensor
        L0 = l * LD
        dve.wait_ge(rows, M.n0["rows"] + ROWS)
        fr, fi = (x[:, L0:L0 + LD].unsqueeze(2).broadcast_to([128, LD, GH]) for x in (cfR, cfI))
        for a, b, o, op in ((0, 1, BbR, ALU.subtract), (1, 0, BbI, ALU.add)):
            t1, t2 = (gt[:, 1, i * 4:i * 4 + 4, :].rearrange("p a c -> p (a c)").rearrange("p (t h) -> p t h", h=GH)
                      for i in range(2))
            dlink(dve, tt(t1, brow[:, a], fr, ALU.mult))
            dlink(dve, tt(t2, brow[:, b], fi, ALU.mult))
            dsync(dve)
            dlink(dve, tt(o[:], t1, t2, op))
            dsync(dve)
        dve.wait_ge(ct, M.n0["ct"] + 1)

        def four(x, t0):
            return x[:, t0:t0 + QP, :].unsqueeze(2).broadcast_to([128, QP, T8, GH])

        def powers(t, k0, k1, t0):
            v = t[:, k0:k1 + 1, L0 + t0:L0 + t0 + QP] if k1 > k0 else t[:, k0:(k1 - 1 if k1 else None):-1, L0 + t0:L0 + t0 + QP]
            return v.rearrange("p k t -> p t k").unsqueeze(3).broadcast_to([128, QP, T8, GH])

        def tiles(x, a, d):
            return x[:, a, d * QP:(d + 1) * QP, :].rearrange("p t (k h) -> p t k h", h=GH)

        def state_in(q):
            if q:
                dve.wait_ge(vt_ps, M.n0["vt_ps"] + q)
                dve.wait_ge(w_made, M.n0["w_made"] + q)
            for d, (k0, k1) in enumerate(((T8 - 1, 0), (0, T8 - 1))):
                t0 = d * NPAIR + q * QP
                br, bi = four(BbR, t0), four(BbI, t0)
                pr, pi = powers(LkR, k0, k1, t0), powers(LkI, k0, k1, t0)
                for x, y, o, op in ((br, bi, 0, ALU.subtract), (bi, br, 1, ALU.add)):
                    dsync(dve)
                    dlink(dve, tt(tiles(gt, 0, d), x, pr, ALU.mult))
                    dlink(dve, tt(tiles(gt, 1, d), y, pi, ALU.mult))
                    dsync(dve)
                    ins = tt(tiles(V, o, d), tiles(gt, 0, d), tiles(gt, 1, d), op)
                    if d == 1 and o == 1:
                        ins.then_inc(v_made, 1)
                    else:
                        dlink(dve, ins)

        def state_out(q):
            if q:
                dve.wait_ge(gen_store, M.n0["gen_store"] + 48 * q)
                dve.wait_ge(tz_ps, M.n0["tz_ps"] + q)
            dve.wait_ge(v_made, M.n0["v_made"] + q + 1)
            for d, (k0, k1) in enumerate(((1, T8), (T8, 1))):
                t0 = d * NPAIR + q * QP
                cr, ci = four(CTr, t0), four(CTi, t0)
                pr, pi = powers(LkR, k0, k1, t0), powers(LkI, k0, k1, t0)
                for x, y, o, op in ((cr, ci, 0, ALU.add), (ci, cr, 1, ALU.subtract)):
                    dsync(dve)
                    dlink(dve, tt(tiles(gt, 0, d), x, pr, ALU.mult))
                    dlink(dve, tt(tiles(gt, 1, d), y, pi, ALU.mult))
                    dsync(dve)
                    ins = tt(tiles(W, o, d), tiles(gt, 0, d), tiles(gt, 1, d), op)
                    if d == 1 and o == 1:
                        ins.then_inc(w_made, 1)
                    else:
                        dlink(dve, ins)

        for q in range(HC):
            state_in(q)
            split_lo(dve, M.base + 2 * q + 3)
            state_out(q)
            split_lo(dve, M.base + 2 * q + 4)

        dve.wait_ge(u_store, M.n0["u_store"] + 16 * HC)
        nb = 6 - tok0 // 128

        def channels(n):
            dve.wait_ge(pq_ps, M.n0["pq_ps"] + n + 1)
            if n >= 2:
                dve.wait_ge(f_ps, M.n0["f_ps"] + n - 1)
            nc.vector.tensor_copy(PQ[:, n % 2, 6 - nb:6].rearrange("p b a d -> p (b a d)"),
                                  ps[:, 2:2 + nb // 2, :].rearrange("p b c -> p (b c)")).then_inc(pq, 1)

        def fourier_rest(n):
            bl, bc = (5, 6) if n % 2 == 0 else (7, 0)
            dve.wait_ge(f_hi, M.n0["f_hi"] + n + 1)
            for t0, t1, v in token_segments(tok0):
                src = ps[:, bl, 0:SEQ] if v == LAT else ps[:, bc, 0:CTX]
                ins = tt(hL[:, HC + n, t0:t1], src, hH[:, HC + n, t0:t1].bitcast(f32), ALU.subtract)
            ins.then_inc(f_lo, 1)

        def turn(q):
            s = q % 2
            dve.wait_ge(b_ps, M.n0["b_ps"] + q + 1)
            if q:
                dve.wait_ge(states, M.n0["states"] + q)
            if q == 1:
                dve.wait_ge(w_lo, M.base + 10)
            if q < 2:
                for x in states_of(M, q):
                    nc.vector.memset(x[:, 0:QP, 0:1], 0.0)
                    dlink(dve, nc.vector.memset(x[:, QP:QT, CCH - 1:CCH], 0.0))
            if q >= 2:
                dve.wait_ge(states_im, M.n0["states_im"] + q - 1)
            segs = [(0, 0, NCH, slice(0, NCH)), (1, 0, CCH, slice(CCH - 1, None, -1)), (1, CCH, NCH, slice(NCH - 1, CCH - 1, -1))]
            for d, j0, j1, cols in segs:
                src = [ps[:, state_bank(q) + 2 * a + d, 0:QP * NCH].rearrange("p (t c) -> p t c", c=NCH)[:, :, cols]
                       for a in range(2)]
                ts = slice(d * QP, (d + 1) * QP)
                er, ei = Es[s][:, 0, ts, j0:j1], Es[s][:, 1, ts, j0:j1]
                for o, a, e in ((za, 0, er), (zb, 1, ei), (zc, 1, er), (zd, 0, ei)):
                    ins = tt(o[:, ts, j0:j1], src[a], e, ALU.mult)
                    last = d == 1 and j0 == CCH and o is zd
                    if last:
                        ins.then_inc(b_read, 1)
                    else:
                        dlink(dve, ins)
            dsync(dve)
            dve.wait_ge(b_read, M.n0["b_read"] + q + 1)
            dlink(dve, tt(za[:], za[:], zb[:], ALU.add))
            dlink(dve, tt(zc[:], zc[:], zd[:], ALU.subtract))
            dsync(dve)
            for t in range(QT):
                col = L0 + (t // QP) * NPAIR + q * QP + t % QP
                decay = r8[:, col:col + 1].broadcast_to([128, NCH])
                dlink(dve, nc.vector.tensor_tensor_scan(zb[:, t, :], decay, za[:, t, :], 0.0, ALU.mult, ALU.add))
                ins = nc.vector.tensor_tensor_scan(zd[:, t, :], decay, zc[:, t, :], 0.0, ALU.mult, ALU.add)
                if t < QT - 1:
                    dlink(dve, ins)
                else:
                    ins.then_inc(scanned, 1)

        def turn_back(q, part, x, y, op, last):
            s = q % 2
            o = states_of(M, q)[part]
            dve.wait_ge(scanned, M.n0["scanned"] + q + 1)
            if q >= 2:
                dve.wait_ge(y_ps, M.n0["y_ps"] + q - 1)
            dsync(dve)
            dlink(dve, tt(za[:], x[:], Es[s][:, 0], ALU.mult))
            dlink(dve, tt(zc[:], y[:], Es[s][:, 1], ALU.mult))
            dsync(dve)
            for d, j0, j1, cols in STATE_SEGS:
                ts = slice(d * QP, (d + 1) * QP)
                ins = tt(o[:, ts, cols], za[:, ts, j0:j1], zc[:, ts, j0:j1], op)
                if last and d == 1 and j0:
                    ins.then_inc(states, 1)
                else:
                    dlink(dve, ins)

        def skip(q):
            if q == 0:
                dve.wait_ge(u_back, M.n0["u_back"] + 16)
            dve.wait_ge(y_back, M.n0["y_back"] + 16 * QG * (q + 1))
            yp = YP[:, 0:T].rearrange("p (t c) -> p t c", t=T8)
            stt(yp, UP2[:, q, :, c0:NCH], skipD[:, l * HC + q:l * HC + q + 1], yp, ALU.mult, ALU.add)\
                .then_inc(y_sum, 1)

        channels(0)
        channels(1)
        fourier_rest(0)
        channels(2)
        fourier_rest(1)
        turn(0)
        turn_back(0, 0, zb, zd, ALU.subtract, False)
        channels(3)
        fourier_rest(2)
        turn_back(0, 1, zd, zb, ALU.add, True)
        fourier_rest(3)
        for q in range(1, HC):
            turn(q)
            if q >= 2:
                skip(q - 2)
            turn_back(q, 0, zb, zd, ALU.subtract, True)
        skip(HC - 2)

        def rest_g(m):
            dve.wait_ge(g_hi, M.n0["g_hi"] + m + 1)
            tt(gL[:, m, 0:T], G[:, m, 0:T], gH[:, m, 0:T].bitcast(f32), ALU.subtract).then_inc(g_lo, 1)

        for m in range(HC - 1):
            rest_g(m)
        skip(HC - 1)
        rest_g(HC - 1)

        def times_gate(m):
            dve.wait_ge(sig, M.n0["sig"] + m + 1)
            if m >= 2:
                dve.wait_ge(cat_hi, M.n0["cat_hi"] + m - 1)
                dve.wait_ge(cat_lo, M.n0["cat_lo"] + m - 1)
            tt(zt[:, m % 2, 0:T], G[:, m, 0:T], sg2[:, m % 2, 0:T], ALU.mult).then_inc(gated, 1)

        def cat_rest(m):
            dve.wait_ge(cat_hi, M.n0["cat_hi"] + m + 1)
            tt(by_chunk(hL, m, tok0), zt[:, m % 2, 0:T].rearrange("p (t c) -> p t c", t=T8),
               by_chunk(hH, m, tok0).bitcast(f32), ALU.subtract).then_inc(cat_lo, 1)
            if m % 2:
                split_lo(dve, M.base + 8 + m // 2 + 3)

        times_gate(0)
        for m in range(HC):
            if m + 1 < HC:
                times_gate(m + 1)
            cat_rest(m)
        for m in range(KC):
            dve.wait_ge(w_used, M.base + 11 + m)
            nc.vector.tensor_copy(sb_pair(yT[:, m, :], tok0), ps_pair(m % 4, tok0)).then_inc(o_read, 1)
            if m < KC - 1:
                split_lo(dve, M.base + 10 + m + 3)


    def start_sync(sp):
        rows = "l d (q g) p -> (l d q) (g p)"
        sp.dma_start(prow[0:64, 0, :], lam_re.rearrange(rows, g=2)).then_inc(s_par, 16)
        sp.dma_start(prow[64:128, 0, :], lam_im.rearrange(rows, g=2)).then_inc(s_par, 16)
        sp.dma_start(prow[0:96, 1, :], norm_g.rearrange("l i (m p) -> (l i m) p", p=128)).then_inc(s_par, 16)
        for l in range(DEPTH):
            sp.dma_start(prow[0:72, 2 + l, :], b_ada[l].rearrange("(m p) -> m p", p=128)).then_inc(s_par, 16)
        sp.dma_start(prow[0:8, 4, :], c.rearrange("a (m p) -> (a m) p", p=128)).then_inc(s_par, 16)
        sp.dma_start(prow[8:16, 4, :], c_ctx.rearrange("(m p) -> m p", p=128)).then_inc(s_par, 16)
        sp.dma_start(prow[16:24, 4, :], ssm_d.rearrange("l (m p) -> (l m) p", p=128)).then_inc(s_par, 16)
        for h in range(2):
            sp.dma_start(pdt[64 * h:64 * h + 64, 0:2], log_dt.rearrange("l d (q g) -> (l d q) g", g=2)).then_inc(s_par, 16)
        sp.dma_start(posR[:], pos_row).then_inc(s_pos, 16)
        sp.dma_start(posC[:], pos_col).then_inc(s_pos, 16)
        sp.dma_start(xin[:, 0:2, :], ctx_in[0].rearrange("(b p) d -> p b d", p=128)).then_inc(s_xin, 16)
        sp.dma_start(xin[:, 2:6, :], x[0].rearrange("(b p) d -> p b d", p=128)).then_inc(s_xin, 16)

    def start_pool(pool):
        nc.gpsimd.memset(ident[:], 0.0).then_inc(s_id, 1)
        nc.gpsimd.memset(ones[:], 1.0).then_inc(s_id, 1)
        nc.gpsimd.memset(modrow[:], 0.0).then_inc(s_id, 1)
        pool.wait_ge(s_id, 3)
        nc.gpsimd.affine_select(out=ident[:], in_=ident[:], compare_op=ALU.not_equal, fill=1.0, base=0,
                                pattern=[[-1, 128]], channel_multiplier=1).then_inc(s_id, 1)
        nc.gpsimd.memset(ones[:, 1:2], EPS).then_inc(s_id, 1)
        for R in range(FIRST_RIDES):
            if R == 2:
                pool.wait_ge(s_xin, 32)
            if R >= 6:
                pool.wait_ge(ada_used, R - 5)
            pool.dma_start(ada_early[R], ada_source(0, R)).then_inc(ada_first[R % 6], 16)

    def start_tensor(pe):
        pe.wait_ge(s_id, 5)
        pe.wait_ge(s_par, 16 * 10)
        pe.wait_ge(s_dt, 1)
        nc.tensor.transpose(ps[:, 6, 0:128], prow[:, 0, :], ident[:])
        nc.tensor.transpose(ps[:, 6, 128:256], prow[:, 5, :], ident[:])
        nc.tensor.transpose(ps[:, 6, 256:352], prow[0:96, 1, :], ident[0:96, 0:96])
        nc.tensor.transpose(ps[:, 6, 384:408], prow[0:24, 4, :], ident[0:24, 0:24])
        for l in range(DEPTH):
            ins = nc.tensor.transpose(ps[:, 7, 128 * l:128 * l + 72], prow[0:72, 2 + l, :], ident[0:72, 0:72])
        ins.then_inc(s_parps, 1)
        pe.wait_ge(s_xin, 32)
        for m in range(KC):
            if m >= 2:
                pe.wait_ge(s_xctx, m - 1)
                pe.wait_ge(s_xlat, m - 1)
            for b in range(6):
                bank, col = (2 * (m % 2), b * 128) if b < 2 else (2 * (m % 2) + 1, b * 128 - CTX)
                ins = nc.tensor.transpose(ps[:, bank, col:col + 128], xin[:, b, m * 128:(m + 1) * 128], ident[:])
            ins.then_inc(s_xps, 1)
        pe.wait_ge(s_xctx, KC)
        pe.wait_ge(s_xlat, KC)
        pe.wait_ge(s_silu, 2)
        pe.wait_ge(s_parT, 3)
        pe.wait_ge(s_lam, 1)
        pre_tensor(pe, pres[0])
        for R in range(FIRST_RIDES):
            if R >= 4:
                pe.wait_ge(ada_rows, R - 3)
            ada_ride(pe, R, R % 4, 0)
            if R:
                ada_turn(pe, R - 1, 4 + (R - 1) % 2, 128 * ((R - 1) // 2))
        ada_turn(pe, FIRST_RIDES - 1, 4 + (FIRST_RIDES - 1) % 2, 128 * ((FIRST_RIDES - 1) // 2))

    def start_scalar(act):
        act.wait_ge(s_par, 16 * 10)
        nc.scalar.activation(pdt[:, 2:4], pdt[:, 0:2], ACT.Exp).then_inc(s_exp, 1)
        act.wait_ge(s_parps, 1)
        nc.scalar.activation(lamT[:].rearrange("p a c -> p (a c)"), ps[:, 6, 0:256], ACT.Copy).then_inc(s_lam, 1)
        nc.scalar.activation(gT[:], ps[:, 6, 256:352], ACT.Copy).then_inc(s_parT, 1)
        nc.scalar.activation(adaB[:].rearrange("p (l m) -> p l m", l=DEPTH),
                             ps[:, 7, 0:256].rearrange("p (l m) -> p l m", l=DEPTH)[:, :, 0:72], ACT.Copy).then_inc(s_parT, 1)
        nc.scalar.activation(skipD[:], ps[:, 6, 400:408], ACT.Copy).then_inc(s_parT, 1)
        for v in range(2):
            nc.scalar.activation(siluC[:, :, v], ps[:, 6, 384 + 8 * v:392 + 8 * v], ACT.Silu).then_inc(s_silu, 1)
        act.wait_ge(s_lam, 1)
        nc.scalar.activation(lt[:, 0, :], lamT[:, 1, 0:64], ACT.Exp).then_inc(s_trig, 1)
        nc.scalar.activation(r8[:], lamT[:, 1, 0:64], ACT.Exp, scale=float(T8)).then_inc(s_trig, 1)
        act.wait_ge(s_red, 1)
        nc.scalar.activation(lt[:, 3, :], lt[:, 2, :], ACT.Sin).then_inc(s_trig, 1)
        nc.scalar.activation(lt[:, 4, :], lt[:, 2, :], ACT.Sin, scale=0.5).then_inc(s_trig, 1)
        for m in range(KC):
            act.wait_ge(s_xps, m + 1)
            nc.scalar.activation(xT[:, m, 0:CTX], ps[:, 2 * (m % 2), 0:CTX], ACT.Copy).then_inc(s_xctx, 1)
        act.wait_ge(s_xctx, KC)
        square_x(act, pres[0], lambda m: act.wait_ge(s_xlat, m + 1))
        pre_scalar(act, pres[0])
        for n in range(SPLIT_SLOTS):
            split_hi(act, n)
        for R in range(FIRST_RIDES):
            take_rows(act, R, R % 4, 0)
            if R:
                take_turned(act, R - 1, 4 + (R - 1) % 2, 128 * ((R - 1) // 2))
        take_turned(act, FIRST_RIDES - 1, 4 + (FIRST_RIDES - 1) % 2, 128 * ((FIRST_RIDES - 1) // 2))

    def start_vector(dve):
        tt, ts_, stt = nc.vector.tensor_tensor, nc.vector.tensor_scalar, nc.vector.scalar_tensor_tensor
        dve.wait_ge(s_exp, 1)
        tt(prow[:, 5, :].rearrange("p (g s) -> p g s", g=2), prow[:, 0, :].rearrange("p (g s) -> p g s", g=2),
           pdt[:, 2:4].unsqueeze(2).broadcast_to([128, 2, NST]), ALU.mult).then_inc(s_dt, 1)
        dve.wait_ge(s_lam, 1)
        ang = lamT[:, 1, 64:128]

        def d(ins):
            dlink(dve, ins)
            dsync(dve)

        d(ts_(lt[:, 1, :], ang, 1.0 / TWO_PI, MAGIC, ALU.mult, ALU.add))
        d(ts_(lt[:, 1, :], lt[:, 1, :], MAGIC, None, ALU.subtract))
        d(stt(lt[:, 2, :], lt[:, 1, :], -PI_A, ang, ALU.mult, ALU.add))
        d(stt(lt[:, 2, :], lt[:, 1, :], -PI_B, lt[:, 2, :], ALU.mult, ALU.add))
        d(stt(lt[:, 2, :], lt[:, 1, :], -PI_C, lt[:, 2, :], ALU.mult, ALU.add))
        ts_(lt[:, 2, :], lt[:, 2, :], 3.1415925, -3.1415925, ALU.min, ALU.max).then_inc(s_red, 1)
        for m in range(KC):
            dve.wait_ge(s_xps, m + 1)
            if m == 0:
                dve.wait_ge(s_pos, 32)
            rows = SEQ // GRID_W
            if m < 4:
                pos = posR[:, m, :].unsqueeze(2).broadcast_to([128, rows, GRID_W])
            else:
                pos = posC[:, m - 4, :].unsqueeze(1).broadcast_to([128, rows, GRID_W])
            tt(xT[:, m, CTX:TOK].rearrange("p (r c) -> p r c", c=GRID_W),
               ps[:, 2 * (m % 2) + 1, 0:SEQ].rearrange("p (r c) -> p r c", c=GRID_W), pos, ALU.add).then_inc(s_xlat, 1)
        dve.wait_ge(s_trig, 4)
        mag, sn, sh, cs = lt[:, 0, :], lt[:, 3, :], lt[:, 4, :], lt[:, 5, :]
        t0, t1, t2, t3 = (lt[:, 6 + i, :] for i in range(4))
        d(tt(t0, sh, sh, ALU.mult))
        d(ts_(cs, t0, -2.0, 1.0, ALU.mult, ALU.add))
        dlink(dve, nc.vector.memset(LkR[:, 0, :], 1.0))
        dlink(dve, nc.vector.memset(LkI[:, 0, :], 0.0))
        dlink(dve, tt(LkR[:, 1, :], mag, cs, ALU.mult))
        d(tt(LkI[:, 1, :], mag, sn, ALU.mult))

        def product(o_r, o_i, ar, ai, br, bi):
            dlink(dve, tt(t0, ar, br, ALU.mult))
            dlink(dve, tt(t1, ai, bi, ALU.mult))
            dlink(dve, tt(t2, ar, bi, ALU.mult))
            d(tt(t3, ai, br, ALU.mult))
            dlink(dve, tt(o_r, t0, t1, ALU.subtract))
            d(tt(o_i, t2, t3, ALU.add))

        for k in range(2, T8 + 1):
            a, b = (k + 1) // 2, k // 2
            product(LkR[:, k, :], LkI[:, k, :], LkR[:, a, :], LkI[:, a, :], LkR[:, b, :], LkI[:, b, :])
        lr, li = lamT[:, 0, 0:64], lamT[:, 0, 64:128]
        d(ts_(lt[:, 10, :], LkR[:, 1, :], -1.0, None, ALU.add))
        dlink(dve, tt(t0, lr, lr, ALU.mult))
        d(tt(t1, li, li, ALU.mult))
        d(tt(t0, t0, t1, ALU.add))
        d(nc.vector.reciprocal(lt[:, 11, :], t0))
        dlink(dve, ts_(lt[:, 12, :], li, -1.0, None, ALU.mult))
        dsync(dve)
        product(lt[:, 13, :], lt[:, 14, :], lt[:, 10, :], LkI[:, 1, :], lr, lt[:, 12, :])
        dlink(dve, tt(cfR[:], lt[:, 13, :], lt[:, 11, :], ALU.mult))
        dlink(dve, tt(cfI[:], lt[:, 14, :], lt[:, 11, :], ALU.mult))
        product(lt[:, 13, :], lt[:, 14, :], cs, sn, cs, sn)
        product(lt[:, 15, :], lt[:, 16, :], lt[:, 13, :], lt[:, 14, :], lt[:, 13, :], lt[:, 14, :])
        product(lt[:, 13, :], lt[:, 14, :], lt[:, 15, :], lt[:, 16, :], lt[:, 15, :], lt[:, 16, :])
        dlink(dve, tt(t0, lt[:, 13, :], lt[:, 13, :], ALU.mult))
        d(tt(t1, lt[:, 14, :], lt[:, 14, :], ALU.mult))
        d(tt(t0, t0, t1, ALU.add))
        d(ts_(t0, t0, -0.5, 1.5, ALU.mult, ALU.add))
        dlink(dve, tt(P8R[:], lt[:, 13, :], t0, ALU.mult))
        dlink(dve, tt(P8I[:], lt[:, 14, :], t0, ALU.mult))
        dsync(dve)
        for n in range(SPLIT_SLOTS):
            split_lo(dve, n)
        dve.wait_ge(s_parT, 3)
        inverse_x(dve, pres[0])
        dve.wait_ge(ada_taken, 2 * KC // RIDE + 1)
        coef_pre(dve, pres[0])
        pre_vector(dve, pres[0])

    def end_tensor(pe, N):
        wait_x(pe, N, POOL_CHUNKS[-1])
        wait_x(pe, N, DVE_CHUNKS[-1])
        for b in range(4):
            if b >= 2:
                pe.wait_ge(s_ocp, b - 1)
            for m in range(KC):
                bank = 4 + 2 * (b % 2) + m // 4
                ins = nc.tensor.transpose(ps[:, bank, (m % 4) * 128:(m % 4) * 128 + 128],
                                          xT[:, m, CTX + b * 128:CTX + (b + 1) * 128], ident[:])
            ins.then_inc(s_ops, 1)

    def end_scalar(act, N):
        for b in range(4):
            act.wait_ge(s_ops, b + 1)
            bank = 4 + 2 * (b % 2)
            nc.scalar.activation(ostage[:, b, :], ps[:, bank:bank + 2, :].rearrange("p b c -> p (b c)"), ACT.Copy)\
                .then_inc(s_ocp, 1)

    def end_sync(sp):
        for b in range(4):
            sp.wait_ge(s_ocp, b + 1)
            sp.dma_start(out[0, b * 128:(b + 1) * 128, :], ostage[:, b, :]).then_inc(s_out, 16)
        sp.wait_ge(s_out, 64)
        for M in (M0, M1):
            sp.wait_ge(u_store, M.n0["u_store"] + 16 * HC)
            sp.wait_ge(gen_store, M.n0["gen_store"] + 48 * HC)
            sp.wait_ge(e_store, M.n0["e_store"] + 16 * HC)
            sp.wait_ge(y_store, M.n0["y_store"] + 16 * HC)

    with stack:
        block = stack.enter_context(nc.Block())

        @block.sync
        def _(sp):
            start_sync(sp)
            for (kind, S, _, _), pre in zip(plan, pres):
                (ffn_sync if kind == "ffn" else lambda e, s: mix_sync(e, s, pre))(sp, S)
            end_sync(sp)

        @block.gpsimd
        def _(pool):
            start_pool(pool)
            for (kind, S, N, nxt), pre in zip(plan, pres):
                if kind == "mix":
                    mix_pool(pool, S, pre)
                add_squares(pool, N)
                post_pool(pool, N)

        @block.tensor
        def _(pe):
            start_tensor(pe)
            for (kind, S, N, nxt), pre in zip(plan, pres):
                (ffn_tensor if kind == "ffn" else mix_tensor)(pe, S, pre)
                post_tensor(pe, N, S)
                if nxt:
                    pre_tensor(pe, nxt)
            end_tensor(pe, plan[-1][2])

        @block.scalar
        def _(act):
            start_scalar(act)
            add_shift(act, pres[0])
            for kind, S, N, nxt in plan:
                (ffn_scalar if kind == "ffn" else mix_scalar)(act, S, N)
                post_scalar(act, N, S)
                if nxt:
                    square_x(act, nxt, lambda m: wait_x(act, N, m))
                    pre_scalar(act, nxt)
                    add_shift(act, nxt)
            end_scalar(act, plan[-1][2])

        @block.vector
        def _(dve):
            start_vector(dve)
            for (kind, S, N, nxt), pre in zip(plan, pres):
                if kind == "ffn":
                    ffn_vector(dve, S)
                else:
                    mix_vector(dve, S, pre)
                post_vector(dve, N, S)
                if nxt:
                    coef_pre(dve, nxt)
                    inverse_x(dve, nxt)
                    pre_vector(dve, nxt)


_INS = ['x', 'c', 'ctx', 'c_ctx', 'w_ada', 'b_ada', 'norm_g', 'ffn1_gu', 'ffn1_down', 'ffn2_gu', 'ffn2_down',
        'w_in', 'w_out', 'ssm_lam_re', 'ssm_lam_im', 'ssm_log_dt', 'ssm_b_re', 'ssm_b_im', 'ssm_c_re', 'ssm_c_im',
        'ssm_d', 'w_glu', 'w_fmix']


def shape_tables():
    quarter = D // 4
    omega = (np.float32(1.0) / (np.float32(10000.0) ** (np.arange(quarter, dtype=np.float32) / np.float32(quarter))))
    omega = omega.astype(np.float32)

    def code(n):
        ang = (np.arange(n, dtype=np.float32)[:, None] * omega[None, :]).astype(np.float32)
        enc = np.concatenate([np.sin(ang), np.cos(ang)], axis=-1).astype(np.float32)
        return np.ascontiguousarray(enc.T.reshape(4, 128, n).transpose(1, 0, 2))

    def dft(n):
        a = np.outer(np.arange(n), np.arange(n)) % n * (2 * np.pi / n)
        return np.cos(a) / np.sqrt(n), np.sin(a) / np.sqrt(n)

    def rows(m):
        n = m.shape[0]
        return m.reshape(n // 128, 128, n).transpose(1, 0, 2)

    cl, sl = dft(SEQ)
    cc, sc = dft(CTX)
    ch, sh = dft(128)
    lat = np.stack([rows(cl), rows(-sl)])
    cx = np.stack([rows(cc), rows(-sc)], axis=1)
    hd = np.stack([ch, sh], axis=1)
    return {"pos_row": code(SEQ // GRID_W), "pos_col": code(GRID_W), "dft_lat": lat, "dft_ctx": cx, "dft_head": hd}


def kernel(**inputs):
    import concourse.bacc as bacc
    from concourse.bass_utils import run_bass_kernel_spmd

    nc = bacc.Bacc("TRN2", target_bir_lowering=False, num_devices=1)
    arrays, args = {}, []
    tables = {k: np.ascontiguousarray(v, dtype=np.float32) for k, v in shape_tables().items()}
    for name in _INS + list(tables):
        a = np.ascontiguousarray(inputs[name]) if name in _INS else tables[name]
        arrays[f"in_{name}_dram"] = a
        args.append(nc.dram_tensor(f"in_{name}_dram", a.shape, mybir.dt.from_np(a.dtype), kind="ExternalInput").ap())
    args.append(nc.dram_tensor("out_0_dram", (1, SEQ, D), f32, kind="ExternalOutput").ap())
    build(nc, *args)
    r = run_bass_kernel_spmd(nc, [arrays], core_ids=[0])
    return r.results[0]["out_0_dram"]
```
